# Optimizing a Trainium2 kernel written in Bass

```python
import math
import jax, jax.numpy as jnp
from jax import lax
import numpy as np

D_MODEL = 1024
BATCH = 1
SEQ = 256
DEPTH = 2

CHUNK = 64
Q_BLOCK = 128
EPS = 1e-6
NEG = -1e30

FOX_HEADS = 4
FOX_DIM = 64
DIFF_HEADS = 4
DIFF_QK = 64
DIFF_V = 2 * DIFF_QK
MLA_HEADS = 4
MLA_NOPE = 64
MLA_ROPE = 32
MLA_V = 64
MLA_Q_RANK = 256
MLA_KV_RANK = 128
ROPE_THETA = 10000.0
D_FF = 2816
CONV_W = 3

MIX_WIDTH = FOX_HEADS * FOX_DIM + DIFF_HEADS * DIFF_V + MLA_HEADS * MLA_V
IN_SIZES = (FOX_HEADS * FOX_DIM, FOX_HEADS * FOX_DIM, FOX_HEADS * FOX_DIM, FOX_HEADS,
            DIFF_HEADS * 2 * DIFF_QK, DIFF_HEADS * 2 * DIFF_QK, DIFF_HEADS * DIFF_V,
            MLA_Q_RANK, MLA_KV_RANK, MLA_ROPE)
IN_COLS = sum(IN_SIZES)


def rmsnorm(x, g):
    xf = x.astype(jnp.float32)
    y = xf * lax.rsqrt(jnp.mean(xf * xf, axis=-1, keepdims=True) + EPS)
    return (y * g.astype(jnp.float32)).astype(x.dtype)

def to_heads(t, h):
    b, s, _ = t.shape
    return t.reshape(b, s, h, -1).transpose(0, 2, 1, 3)

def merge_heads(t):
    b, h, s, d = t.shape
    return t.transpose(0, 2, 1, 3).reshape(b, s, h * d)

def rope(x, pos):
    half = x.shape[-1] // 2
    inv = 1.0 / (ROPE_THETA ** (jnp.arange(half, dtype=jnp.float32) / half))
    ang = pos[:, None] * inv[None, :]
    cos, sin = jnp.cos(ang), jnp.sin(ang)
    xf = x.astype(jnp.float32)
    x1, x2 = xf[..., :half], xf[..., half:]
    return jnp.concatenate([x1 * cos - x2 * sin, x1 * sin + x2 * cos], axis=-1).astype(x.dtype)

def block_attention(q, k, v, bias_fn, scale):
    b, h, s, _ = q.shape
    dv = v.shape[-1]
    ki = jnp.arange(s)

    def one(blk):
        start = blk * Q_BLOCK
        qb = lax.dynamic_slice_in_dim(q, start, Q_BLOCK, axis=2)
        qi = start + jnp.arange(Q_BLOCK)
        sc = jnp.einsum('bhqd,bhkd->bhqk', qb, k).astype(jnp.float32) * scale
        p = jax.nn.softmax(sc + bias_fn(qi, ki), axis=-1).astype(v.dtype)
        return jnp.einsum('bhqk,bhkd->bhqd', p, v)

    out = lax.map(one, jnp.arange(s // Q_BLOCK))
    return out.transpose(1, 2, 0, 3, 4).reshape(b, h, s, dv)

def chunk_mask(qi, ki):
    return (ki[None, :] // CHUNK) <= (qi[:, None] // CHUNK)

def fox_group(q, k, v, f_logit, f_bias):
    q, k, v = to_heads(q, FOX_HEADS), to_heads(k, FOX_HEADS), to_heads(v, FOX_HEADS)
    logf = jax.nn.log_sigmoid((f_logit + f_bias).astype(jnp.float32))
    cum = jnp.cumsum(logf, axis=1).transpose(0, 2, 1)

    def bias(qi, ki):
        cq = jnp.take(cum, qi, axis=2)
        d = cq[..., :, None] - cum[..., None, :]
        return jnp.where((ki[None, :] <= qi[:, None])[None, None], d, NEG)

    return merge_heads(block_attention(q, k, v, bias, FOX_DIM ** -0.5))

def diff_group(q, k, v, lq1, lk1, lq2, lk2, norm_g, lam_init):
    q, k, v = to_heads(q, DIFF_HEADS), to_heads(k, DIFF_HEADS), to_heads(v, DIFF_HEADS)
    q1, q2 = q[..., :DIFF_QK], q[..., DIFF_QK:]
    k1, k2 = k[..., :DIFF_QK], k[..., DIFF_QK:]
    slopes = 2.0 ** (-8.0 * jnp.arange(1, DIFF_HEADS + 1, dtype=jnp.float32) / DIFF_HEADS)

    def bias(qi, ki):
        dist = jnp.abs(qi[:, None] - ki[None, :]).astype(jnp.float32)
        alibi = -slopes[:, None, None] * dist[None]
        return jnp.where(chunk_mask(qi, ki)[None], alibi, NEG)[None]

    scale = DIFF_QK ** -0.5
    o1 = block_attention(q1, k1, v, bias, scale)
    o2 = block_attention(q2, k2, v, bias, scale)
    lam = (jnp.exp(jnp.sum(lq1.astype(jnp.float32) * lk1.astype(jnp.float32)))
           - jnp.exp(jnp.sum(lq2.astype(jnp.float32) * lk2.astype(jnp.float32))) + lam_init)
    o = o1 - lam.astype(o1.dtype) * o2
    o = rmsnorm(o, norm_g) * (1.0 - lam_init)
    return merge_heads(o)

def mla_group(c_q, c_kv, k_rope_raw, q_norm_g, w_uq, kv_norm_g, w_ukv, pos):
    q = to_heads(rmsnorm(c_q, q_norm_g) @ w_uq, MLA_HEADS)
    q = jnp.concatenate([q[..., :MLA_NOPE], rope(q[..., MLA_NOPE:], pos)], axis=-1)
    kv = to_heads(rmsnorm(c_kv, kv_norm_g) @ w_ukv, MLA_HEADS)
    k_nope, v = kv[..., :MLA_NOPE], kv[..., MLA_NOPE:]
    k_r = rope(k_rope_raw[:, None], pos)
    k = jnp.concatenate([k_nope, jnp.broadcast_to(k_r, k_nope.shape[:3] + (MLA_ROPE,))], axis=-1)

    def bias(qi, ki):
        return jnp.where(chunk_mask(qi, ki), 0.0, NEG)[None, None]

    return merge_heads(block_attention(q, k, v, bias, (MLA_NOPE + MLA_ROPE) ** -0.5))

def causal_dwconv(u, w, b):
    s = u.shape[1]
    up = jnp.pad(u, ((0, 0), (CONV_W - 1, 0), (0, 0)))
    y = b
    for j in range(CONV_W):
        y = y + up[:, j:j + s, :] * w[j]
    return y

def first_inputs(seed: int = 0) -> dict:
    key = jax.random.key(seed)
    ks = jax.random.split(key, 24)
    n = jax.random.normal
    f32 = jnp.float32
    return {
        'x': n(ks[0], (BATCH, SEQ, D_MODEL), f32),
        'ln1_g': 1.0 + 0.02 * n(ks[1], (DEPTH, D_MODEL), f32),
        'w_in': n(ks[2], (DEPTH, D_MODEL, IN_COLS), f32) * D_MODEL ** -0.5,
        'fgate_b': 2.0 + 0.5 * n(ks[3], (DEPTH, FOX_HEADS), f32),
        'lam_q1': 0.1 * n(ks[4], (DEPTH, DIFF_QK), f32),
        'lam_k1': 0.1 * n(ks[5], (DEPTH, DIFF_QK), f32),
        'lam_q2': 0.1 * n(ks[6], (DEPTH, DIFF_QK), f32),
        'lam_k2': 0.1 * n(ks[7], (DEPTH, DIFF_QK), f32),
        'diff_norm_g': 1.0 + 0.02 * n(ks[8], (DEPTH, DIFF_V), f32),
        'q_norm_g': 1.0 + 0.02 * n(ks[9], (DEPTH, MLA_Q_RANK), f32),
        'w_uq': n(ks[10], (DEPTH, MLA_Q_RANK, MLA_HEADS * (MLA_NOPE + MLA_ROPE)), f32) * MLA_Q_RANK ** -0.5,
        'kv_norm_g': 1.0 + 0.02 * n(ks[11], (DEPTH, MLA_KV_RANK), f32),
        'w_ukv': n(ks[12], (DEPTH, MLA_KV_RANK, MLA_HEADS * (MLA_NOPE + MLA_V)), f32) * MLA_KV_RANK ** -0.5,
        'w_o': n(ks[13], (DEPTH, MIX_WIDTH, D_MODEL), f32) * MIX_WIDTH ** -0.5,
        'ln2_g': 1.0 + 0.02 * n(ks[14], (DEPTH, D_MODEL), f32),
        'w_up': n(ks[15], (DEPTH, D_MODEL, 2 * D_FF), f32) * D_MODEL ** -0.5,
        'conv_w': n(ks[16], (DEPTH, CONV_W, 2 * D_FF), f32) * CONV_W ** -0.5,
        'conv_b': 0.02 * n(ks[17], (DEPTH, 2 * D_FF), f32),
        'w_down': n(ks[18], (DEPTH, D_FF, D_MODEL), f32) * D_FF ** -0.5,
        'final_g': 1.0 + 0.02 * n(ks[19], (D_MODEL,), f32),
    }

def first_block(x, ln1_g, w_in, fgate_b, lam_q1, lam_k1, lam_q2, lam_k2, diff_norm_g,
              q_norm_g, w_uq, kv_norm_g, w_ukv, w_o, ln2_g, w_up, conv_w, conv_b,
              w_down, final_g):
    pos = jnp.arange(x.shape[1], dtype=jnp.float32)
    split_points = np.cumsum(IN_SIZES)[:-1].tolist()
    for i in range(DEPTH):
        lam_init = 0.8 - 0.6 * math.exp(-0.3 * i)
        h = rmsnorm(x, ln1_g[i]) @ w_in[i]
        (fq, fk, fv, ff, dq, dk, dv, c_q, c_kv, k_r) = jnp.split(h, split_points, axis=-1)
        o_fox = fox_group(fq, fk, fv, ff, fgate_b[i])
        o_diff = diff_group(dq, dk, dv, lam_q1[i], lam_k1[i], lam_q2[i], lam_k2[i],
                            diff_norm_g[i], lam_init)
        o_mla = mla_group(c_q, c_kv, k_r, q_norm_g[i], w_uq[i], kv_norm_g[i], w_ukv[i], pos)
        x = x + jnp.concatenate([o_fox, o_diff, o_mla], axis=-1) @ w_o[i]
        up = causal_dwconv(rmsnorm(x, ln2_g[i]) @ w_up[i], conv_w[i], conv_b[i])
        g, u = up[..., :D_FF], up[..., D_FF:]
        x = x + (jax.nn.silu(g) * u) @ w_down[i]
    return rmsnorm(x, final_g)


RET_HEAD_DIM = 128
RET_WIDTH = D_MODEL // 2
RET_HEADS = RET_WIDTH // RET_HEAD_DIM
HGRN_HEAD_DIM = 128
HGRN_WIDTH = D_MODEL - RET_WIDTH
HGRN_HEADS = HGRN_WIDTH // HGRN_HEAD_DIM
MIX_WIDTH_2 = RET_WIDTH + HGRN_WIDTH
IN_WIDTHS = [RET_WIDTH] * 4 + [HGRN_WIDTH] * 5
IN_COLS_2 = sum(IN_WIDTHS)
RET_CHUNK = 128
HGRN_CHUNK = 64
ROPE_BASE = 10000.0
N_EXPERTS = 16
CAPACITY_FACTOR = 2
EXPERT_FF = 1024
NORM_EPS = 1e-6


def rms_normalize(x):
    xf = x.astype(jnp.float32)
    return (xf * lax.rsqrt(jnp.mean(xf * xf, axis=-1, keepdims=True) + NORM_EPS)).astype(x.dtype)

def rms_norm(x, g):
    return rms_normalize(x) * g.astype(x.dtype)

def to_heads_2(t, n_heads):
    b, s, _ = t.shape
    return t.reshape(b, s, n_heads, -1).transpose(0, 2, 1, 3)

def from_heads(t):
    b, h, s, d = t.shape
    return t.transpose(0, 2, 1, 3).reshape(b, s, h * d)

def to_chunks(t, chunk):
    b, h, s, d = t.shape
    return t.reshape(b, h, s // chunk, chunk, d).transpose(2, 0, 1, 3, 4)

def from_chunks(t):
    n, b, h, c, d = t.shape
    return t.transpose(1, 2, 0, 3, 4).reshape(b, h, n * c, d)

def rotary(x, pos):
    half = x.shape[-1] // 2
    inv_freq = ROPE_BASE ** (-jnp.arange(half, dtype=jnp.float32) / half)
    ang = pos.astype(jnp.float32)[:, None] * inv_freq[None, :]
    cos = jnp.cos(ang).astype(x.dtype)
    sin = jnp.sin(ang).astype(x.dtype)
    x1, x2 = x[..., :half], x[..., half:]
    return jnp.concatenate([x1 * cos - x2 * sin, x1 * sin + x2 * cos], axis=-1)

def retention_scan(q, k, v, log_gamma, include_diag):
    b, h, s, dk = q.shape
    dv = v.shape[-1]
    dt = q.dtype
    L = RET_CHUNK
    t = jnp.arange(L, dtype=jnp.float32)
    diff = t[:, None] - t[None, :]
    mask = (diff >= 0) if include_diag else (diff > 0)
    lg = log_gamma[:, None, None]
    intra_decay = jnp.where(mask, jnp.exp(lg * jnp.maximum(diff, 0.0)), 0.0).astype(dt)
    q_decay = jnp.exp(log_gamma[:, None] * (t + 1.0))[:, :, None].astype(dt)
    k_decay = jnp.exp(log_gamma[:, None] * (L - 1.0 - t))[:, :, None].astype(dt)
    chunk_decay = jnp.exp(log_gamma * L)[:, None, None].astype(dt)

    def step(state, inp):
        qc, kc, vc = inp
        scores = jnp.einsum('bhid,bhjd->bhij', qc, kc) * intra_decay
        out = (jnp.einsum('bhij,bhjv->bhiv', scores, vc)
               + jnp.einsum('bhid,bhdv->bhiv', qc * q_decay, state))
        state = chunk_decay * state + jnp.einsum('bhjd,bhjv->bhdv', kc * k_decay, vc)
        return state, out

    state0 = jnp.zeros((b, h, dk, dv), dt)
    _, out = lax.scan(step, state0, (to_chunks(q, L), to_chunks(k, L), to_chunks(v, L)))
    return from_chunks(out)

def hgrn2_scan(q, k, v, log_f):
    b, h, s, dk = q.shape
    dv = v.shape[-1]
    dt = q.dtype
    L = HGRN_CHUNK
    causal = jnp.tril(jnp.ones((L, L), dtype=bool))[:, :, None]

    def step(state, inp):
        qc, kc, vc, gc = inp
        cum = jnp.cumsum(gc, axis=2)
        rel = jnp.exp(jnp.where(causal, cum[:, :, :, None, :] - cum[:, :, None, :, :], -jnp.inf)).astype(dt)
        scores = jnp.einsum('bhtd,bhsd,bhtsd->bhts', qc, kc, rel)
        out = (jnp.einsum('bhts,bhsv->bhtv', scores, vc)
               + jnp.einsum('bhtd,bhdv->bhtv', qc * jnp.exp(cum).astype(dt), state))
        cum_end = cum[:, :, -1, :]
        k_to_end = kc * jnp.exp(cum_end[:, :, None, :] - cum).astype(dt)
        state = (jnp.exp(cum_end).astype(dt)[..., None] * state
                 + jnp.einsum('bhsd,bhsv->bhdv', k_to_end, vc))
        return state, out

    state0 = jnp.zeros((b, h, dk, dv), dt)
    _, out = lax.scan(step, state0, (to_chunks(q, L), to_chunks(k, L), to_chunks(v, L), to_chunks(log_f, L)))
    return from_chunks(out)

def flip_seq(t):
    return jnp.flip(t, axis=2)

def hybrid_mixer(xn, w_in, ret_g, hgrn_g, w_out, lb):
    b, s, _ = xn.shape
    dt = xn.dtype
    proj = xn @ w_in
    splits = np.cumsum(IN_WIDTHS)[:-1].tolist()
    rq, rk, rv, rg, hq, hf_fwd, hf_bwd, hi, hg = jnp.split(proj, splits, axis=-1)

    pos = jnp.arange(s)
    q = rotary(to_heads_2(rq, RET_HEADS), pos)
    k = rotary(to_heads_2(rk, RET_HEADS), pos) * (RET_HEAD_DIM ** -0.5)
    v = to_heads_2(rv, RET_HEADS)
    log_gamma = jnp.log1p(-(2.0 ** (-5.0 - jnp.arange(RET_HEADS, dtype=jnp.float32))))
    r_out = (retention_scan(q, k, v, log_gamma, True)
             + flip_seq(retention_scan(flip_seq(q), flip_seq(k), flip_seq(v), log_gamma, False)))
    r_out = from_heads(rms_normalize(r_out)) * ret_g.astype(dt) * jax.nn.silu(rg)

    q2 = jax.nn.silu(to_heads_2(hq, HGRN_HEADS)) * (HGRN_HEAD_DIM ** -0.5)
    v2 = to_heads_2(hi, HGRN_HEADS)

    def forget(z):
        z = z.astype(jnp.float32)
        if lb is None:
            return jax.nn.log_sigmoid(z), jax.nn.sigmoid(-z).astype(dt)
        lbh = lb.astype(jnp.float32).reshape(HGRN_HEADS, 1, HGRN_HEAD_DIM)
        f = lbh + (1.0 - lbh) * jax.nn.sigmoid(z)
        return jnp.log(f), ((1.0 - lbh) * jax.nn.sigmoid(-z)).astype(dt)

    logf_f, k_f = forget(to_heads_2(hf_fwd, HGRN_HEADS))
    logf_b, k_b = forget(to_heads_2(hf_bwd, HGRN_HEADS))
    h_out = (hgrn2_scan(q2, k_f, v2, logf_f)
             + flip_seq(hgrn2_scan(flip_seq(q2), flip_seq(k_b), flip_seq(v2), flip_seq(logf_b))))
    h_out = rms_norm(from_heads(h_out), hgrn_g) * jax.nn.silu(hg)

    return jnp.concatenate([r_out, h_out], axis=-1) @ w_out

def expert_choice_ffn(xn, w_router, w_gate, w_up, w_down):
    b, s, d = xn.shape
    cap = CAPACITY_FACTOR * s // N_EXPERTS
    affinity = jax.nn.softmax((xn @ w_router).astype(jnp.float32), axis=-1)
    gate, idx = lax.top_k(jnp.swapaxes(affinity, 1, 2), cap)
    xe = jax.vmap(lambda xb, ib: xb[ib])(xn, idx)
    hid = (jax.nn.silu(jnp.einsum('becd,edf->becf', xe, w_gate))
           * jnp.einsum('becd,edf->becf', xe, w_up))
    ye = jnp.einsum('becf,efd->becd', hid, w_down) * gate[..., None].astype(xn.dtype)
    return jax.vmap(lambda yb, ib: jnp.zeros((s, d), yb.dtype).at[ib.reshape(-1)].add(yb.reshape(-1, d)))(ye, idx)

def second_inputs(seed: int = 0) -> dict:
    key = jax.random.key(seed)
    ks = jax.random.split(key, 14)
    f32 = jnp.float32
    x = jax.random.normal(ks[0], (BATCH, SEQ, D_MODEL), f32)
    norm1_g = 1.0 + 0.02 * jax.random.normal(ks[1], (DEPTH, D_MODEL), f32)
    w_in = jax.random.normal(ks[2], (DEPTH, D_MODEL, IN_COLS_2), f32) * D_MODEL ** -0.5
    ret_norm_g = 1.0 + 0.02 * jax.random.normal(ks[3], (DEPTH, RET_WIDTH), f32)
    hgrn_norm_g = 1.0 + 0.02 * jax.random.normal(ks[4], (DEPTH, HGRN_WIDTH), f32)
    w_out = jax.random.normal(ks[5], (DEPTH, MIX_WIDTH_2, D_MODEL), f32) * MIX_WIDTH_2 ** -0.5
    lower_bounds = 0.1 * jax.random.normal(ks[6], (DEPTH, HGRN_WIDTH), f32)
    norm2_g = 1.0 + 0.02 * jax.random.normal(ks[7], (DEPTH, D_MODEL), f32)
    w_router = jax.random.normal(ks[8], (DEPTH, D_MODEL, N_EXPERTS), f32) * D_MODEL ** -0.5
    w_gate = jax.random.normal(ks[9], (DEPTH, N_EXPERTS, D_MODEL, EXPERT_FF), f32) * D_MODEL ** -0.5
    w_up = jax.random.normal(ks[10], (DEPTH, N_EXPERTS, D_MODEL, EXPERT_FF), f32) * D_MODEL ** -0.5
    w_down = jax.random.normal(ks[11], (DEPTH, N_EXPERTS, EXPERT_FF, D_MODEL), f32) * EXPERT_FF ** -0.5
    final_norm_g = 1.0 + 0.02 * jax.random.normal(ks[12], (D_MODEL,), f32)
    return {"x": x, "norm1_g": norm1_g, "w_in": w_in, "ret_norm_g": ret_norm_g,
            "hgrn_norm_g": hgrn_norm_g, "w_out": w_out, "lower_bounds": lower_bounds,
            "norm2_g": norm2_g, "w_router": w_router, "w_gate": w_gate, "w_up": w_up,
            "w_down": w_down, "final_norm_g": final_norm_g}

def second_block(x, norm1_g, w_in, ret_norm_g, hgrn_norm_g, w_out, lower_bounds,
              norm2_g, w_router, w_gate, w_up, w_down, final_norm_g):
    lbs = jax.nn.softmax(lower_bounds.astype(jnp.float32), axis=0)
    lbs = jnp.cumsum(lbs, axis=0) - lbs[0]
    h = x
    for layer in range(DEPTH):
        lb = lbs[layer] if layer > 0 else None
        h = h + hybrid_mixer(rms_norm(h, norm1_g[layer]), w_in[layer], ret_norm_g[layer],
                             hgrn_norm_g[layer], w_out[layer], lb)
        h = h + expert_choice_ffn(rms_norm(h, norm2_g[layer]), w_router[layer],
                                  w_gate[layer], w_up[layer], w_down[layer])
    return rms_norm(h, final_norm_g)


def setup_inputs(seed=0):
    out = dict(first_inputs(seed))
    for name, value in second_inputs(seed + 1).items():
        if name != "x":
            out[name + "_2"] = value
    return out


def reference(
    x, ln1_g, w_in, fgate_b, lam_q1, lam_k1, lam_q2, lam_k2, diff_norm_g, q_norm_g, w_uq,
    kv_norm_g, w_ukv, w_o, ln2_g, w_up, conv_w, conv_b, w_down, final_g, norm1_g_2, w_in_2,
    ret_norm_g_2, hgrn_norm_g_2, w_out_2, lower_bounds_2, norm2_g_2, w_router_2, w_gate_2,
    w_up_2, w_down_2, final_norm_g_2,
):
    x = first_block(
        x, ln1_g, w_in, fgate_b, lam_q1, lam_k1, lam_q2, lam_k2, diff_norm_g, q_norm_g, w_uq,
        kv_norm_g, w_ukv, w_o, ln2_g, w_up, conv_w, conv_b, w_down, final_g,
    )
    return second_block(
        x, norm1_g_2, w_in_2, ret_norm_g_2, hgrn_norm_g_2, w_out_2, lower_bounds_2, norm2_g_2,
        w_router_2, w_gate_2, w_up_2, w_down_2, final_norm_g_2,
    )


_drawn_inputs = setup_inputs


def setup_inputs(seed=0):
    import zlib

    import numpy as np

    out = dict(_drawn_inputs(seed))
    spreads = {}
    factors = {'q_norm_g': 8.0,
     'kv_norm_g': 6.026,
     'ret_norm_g_2': 3.542,
     'hgrn_norm_g_2': 3.692,
     'lower_bounds_2': 5.873,
     'norm2_g_2': 2.732,
     'final_norm_g_2': 2.824}
    for name, (base, spread) in spreads.items():
        noise = np.random.default_rng([zlib.crc32(name.encode()), seed]).standard_normal(out[name].shape)
        drawn = base * np.exp(spread * noise) if base else spread * noise
        out[name] = __import__('jax').numpy.asarray(drawn.astype(out[name].dtype))
    for name, factor in factors.items():
        out[name] = (out[name] * factor).astype(out[name].dtype)
    return out
```

```python
import math
from contextlib import ExitStack

import numpy as np

import concourse.bass as bass
from concourse import mybir

F32 = mybir.dt.float32
F32R = mybir.dt.float32r
U8 = mybir.dt.uint8
ALU = mybir.AluOpType
ACT = mybir.ActivationFunctionType
AX = mybir.AxisListType

P = 128
D = 1024
KD = D // P
S = 256
TT = S // P
DEPTH = 2
EPS = 1e-6
NEG = -1e30

FOX_H, FOX_D = 4, 64
DIFF_H, DIFF_QK, DIFF_V = 4, 64, 128
MLA_H, NOPE, ROPE, MLA_V = 4, 64, 32, 64
MLA_QK = NOPE + ROPE
Q_RANK, KV_RANK = 256, 128
D_FF = 2816
FF_CH = D_FF // P
FF_STEPS = FF_CH // 2

SLOTS, SLOTS_1 = 12, 6
SLOT_W = 8 * 256
ARENA = 21456
USES_1 = 48
FF_USE = 15

IN_BLOCKS = [("cq", 2308, 256), ("ckv", 2564, 160), ("fv", 512, 256), ("fq", 0, 256), ("fk", 256, 256),
             ("dq0", 772, 256), ("dq1", 1028, 256), ("dk0", 1284, 256), ("dk1", 1540, 256),
             ("dv0", 1796, 256), ("dv1", 2052, 256)]
IN_OWNER = ["dve", "dve", "dve", "act", "dve", "act", "act", "dve", "dve", "act", "dve"]
IN_COUNT = [IN_OWNER[:i + 1].count(IN_OWNER[i]) for i in range(len(IN_BLOCKS))]
N_ACT_IN, N_DVE_IN = IN_OWNER.count("act"), IN_OWNER.count("dve")

UNITS = ([("diff", h, i) for h in range(DIFF_H) for i in range(2)]
         + [("fox", h, 0) for h in range(FOX_H)] + [("mla", h, 0) for h in range(MLA_H)])
NU = len(UNITS)
MIX_COL = {"fox": 0, "diff": FOX_H * FOX_D, "mla": FOX_H * FOX_D + DIFF_H * DIFF_V}
SPAN = 3 * P

C_W0, C_W1, C_LN1, C_LN2, C_QN, C_KVN, C_FG = 0, 44, 88, 96, 104, 106, 107
C_W2, C_CB, C_SECOND, C_DG, C_NLAM, NPAR = 128, 172, 216, 256, 384, 385


HEADS, HD = 4, 128
WIDTH = HEADS * HD
EXPERTS, CAP, EFF = 16, 2 * S // 16, 1024
GROUP = P // CAP
N_GROUPS = EXPERTS // GROUP
F_STEPS = EFF // 256
TINY = 2.0 ** -60
LOG_TINY = 60.0 * math.log(2.0)
IN2_BLOCKS = [("zf0", 2560), ("zf1", 2816), ("zb0", 3072), ("zb1", 3328), ("hq0", 2048), ("hq1", 2304),
              ("rq0", 0), ("rq1", 256), ("rk0", 512), ("rk1", 768), ("rv0", 1024), ("rv1", 1280),
              ("hi0", 3584), ("hi1", 3840), ("rg0", 1536), ("rg1", 1792), ("hg0", 4096), ("hg1", 4352)]
TOKEN_MAJOR = ("rv", "hi", "rg", "hg")
HALVES = [128, 64, 32, 16, 8, 4, 2, 1]
LEVELS = len(HALVES) + 1
ITEMS = ([("in", i) for i in range(10)] + [("rot", i) for i in range(4)] + [("in", i) for i in range(10, 18)]
         + [("score", h) for h in range(HEADS)])
C2_N1, C2_N2, C2_LB, C2_OML, C2_FLAG, NPAR2 = 0, 8, 16, 20, 24, 28


def emptied_by(n):
    owner = ["act" if kind == "in" else "dve" for kind, _ in ITEMS]
    return owner[n], owner[:n + 1].count(owner[n])


def ff_use(v):
    v -= FF_USE
    if v < 2:
        return 0, v
    if v == USES_1 - FF_USE - 1:
        return FF_STEPS - 1, 2
    j, what = divmod(v - 2, 3)
    return (j, 2) if what == 2 else (j + 1, what)


FF_OF = {ff_use(v): v for v in range(FF_USE, USES_1)}


def second_constants():
    parts, where, at = [], {}, 0

    def put(name, rows):
        nonlocal at
        parts.append(rows.astype(np.float32))
        where[name] = (at, rows.shape[1])
        at += rows.shape[1]

    half = HD // 2
    inv = (np.float32(10000.0) ** (-np.arange(half, dtype=np.float32) / np.float32(half))).astype(np.float32)
    ang = (np.arange(S, dtype=np.float32)[None, :] * inv[:, None]).astype(np.float32)
    put("cos", np.concatenate([np.cos(ang)] * 2))
    put("sin", np.concatenate([np.sin(ang)] * 2))
    turn = np.zeros((HD, HD), np.float32)
    for i in range(half):
        turn[half + i, i] = -1.0
        turn[i, half + i] = 1.0
    put("turn", turn)
    m, n = np.arange(P)[:, None], np.arange(3 * P)[None, :] - P
    for h in range(HEADS):
        gamma = np.log1p(-(2.0 ** (-5.0 - h)))
        put(f"decay{h}", np.exp(gamma * np.abs(n - m)) * HD ** -0.5)
    put("count", np.tile(np.arange(1, CAP + 1), (P, 1)))
    s, t = np.arange(P)[:, None], np.arange(P)[None, :]
    masks = [((s // (2 * h) == t // (2 * h)) & (s // h != t // h)) for h in HALVES[2:]] + [s == t]
    return where, np.concatenate(parts, axis=1), np.concatenate(masks, axis=1).astype(np.uint8)


def rotary_tables(dims, theta, tokens):
    half = dims // 2
    inv = (1.0 / (np.float32(theta) ** (np.arange(half, dtype=np.float32) / np.float32(half)))).astype(np.float32)
    ang = (np.arange(tokens, dtype=np.float32)[None, :] * inv[:, None]).astype(np.float32)
    return np.cos(ang).astype(np.float32), np.sin(ang).astype(np.float32)


def first_constants():
    parts, where, at = [], {}, 0

    def put(name, rows):
        nonlocal at
        full = np.zeros((P, rows.shape[1]), np.float32)
        full[:rows.shape[0]] = rows
        parts.append(full)
        where[name] = (at, rows.shape[1])
        at += rows.shape[1]

    def spans(full):
        return np.concatenate([full[:P, :P], full[P:, :]], axis=1)

    put("ident", np.eye(P, dtype=np.float32))
    q, k = np.arange(S)[:, None], np.arange(S)[None, :]
    put("fox_mask", spans(np.where(k <= q, 0.0, -NEG).astype(np.float32)))
    seen = (k // 64) <= (q // 64)
    put("mla_mask", spans(np.where(seen, 0.0, -NEG).astype(np.float32)))
    for h in range(DIFF_H):
        slope = np.float32(2.0 ** (-8.0 * (h + 1) / DIFF_H))
        put(f"diff_mask{h}", spans(np.where(seen, slope * np.abs(q - k), -NEG).astype(np.float32)))
    cos, sin = rotary_tables(ROPE, 10000.0, S)
    put("cos", np.concatenate([np.ones((NOPE, S), np.float32), cos, cos]))
    put("sin", np.concatenate([np.zeros((NOPE, S), np.float32), sin, sin]))
    turn = np.zeros((MLA_QK, MLA_QK), np.float32)
    for i in range(ROPE // 2):
        turn[NOPE + ROPE // 2 + i, NOPE + i] = -1.0
        turn[NOPE + i, NOPE + ROPE // 2 + i] = 1.0
    put("turn", turn)
    pick = np.zeros((FOX_H, FOX_H, S), np.float32)
    for h in range(FOX_H):
        pick[h, h] = 1.0
    put("pick", pick.reshape(FOX_H, FOX_H * S))
    return where, np.concatenate(parts, axis=1)


def build(nc, w, out):
    ctx = ExitStack()
    with ctx:
        def sb(name, shape, dt=F32):
            return ctx.enter_context(nc.sbuf_tensor(name, shape, dt))

        def sem(name):
            return ctx.enter_context(nc.semaphore(name))

        ring = sb("ring", [P, SLOTS * SLOT_W])
        X = sb("X", [P, TT, D])
        XN = sb("XN", [P, TT, D])
        XT = sb("XT", [P, KD, S])
        arena = sb("arena", [P, ARENA])
        psum = ctx.enter_context(nc.psum_tensor("psum", [P, 8, 512], F32))

        def in_place_of(name, home, at, shape):
            return nc.alloc_sbuf_tensor_at(name, shape, F32R, offset=nc.lookup_mloc(home).addr + 4 * at)

        def split_buffer(name, i, shape):
            return in_place_of(name, ring, (SLOTS_1 + i) * SLOT_W, shape)

        W_BUFS = 3
        W1 = [split_buffer("W1_0", 0, [P, SLOT_W]), split_buffer("W1_1", 1, [P, SLOT_W]), in_place_of("W1_2", XN, 0, [P, SLOT_W])]
        W2 = [split_buffer("W2_0", 2, [P, SLOT_W]), split_buffer("W2_1", 3, [P, SLOT_W]), in_place_of("W2_2", XT, 0, [P, SLOT_W])]
        XT1, XT2 = (split_buffer(f"XT{i + 1}", 4 + i, [P, KD, S]) for i in range(2))

        where1, table1 = first_constants()
        const1 = nc.inline_tensor(table1, "first_constants").ap()

        cursor = [0]

        def place(n):
            at = cursor[0]
            cursor[0] += n
            assert cursor[0] <= ARENA, cursor[0]
            return arena[:, at:at + n]

        def slot(s, n=8 * 256):
            return ring[:, s * SLOT_W:s * SLOT_W + n]

        ss = place(2)
        rs = place(2)
        expo10 = place(10)
        expo = expo10[:, 0:8]
        one = place(1)
        par = place(NPAR)
        par2_all = place(DEPTH * NPAR2).rearrange("p (l n) -> p l n", l=DEPTH)
        par_end = cursor[0]
        cst = place(table1.shape[1])

        def const(name, rows=P):
            at, n = where1[name]
            return cst[0:rows, at:at + n]

        ident = const("ident")
        par_all = place(DEPTH * NPAR).rearrange("p (l n) -> p l n", l=DEPTH)
        wf = place(8 * FOX_H).rearrange("p (k n) -> p k n", k=8)
        wu = place(2 * MLA_H * MLA_QK + MLA_H * (NOPE + MLA_V))
        wuq = wu[:, 0:2 * MLA_H * MLA_QK].rearrange("p (k n) -> p k n", k=2)
        wukv = wu[:, 2 * MLA_H * MLA_QK:]
        first_free = cursor[0]

        rows = place(DEPTH * 2 * P).rearrange("p (l t n) -> p l t n", l=DEPTH, t=2)
        lamv = place(DEPTH * 4 * DIFF_QK).rearrange("p (l i n) -> p l i n", l=DEPTH, i=4)
        lamp = place(DIFF_QK)
        lams = place(2 * DEPTH)
        lame = place(2 * DEPTH)

        cursor[0] = first_free
        fqT, fkT = (place(2 * S).rearrange("p (m s) -> p m s", m=2) for _ in range(2))
        fv = place(2 * S).rearrange("p (t n) -> p t n", t=TT)
        dqT, dkT = (place(4 * S).rearrange("p (m s) -> p m s", m=4) for _ in range(2))
        dv = place(4 * S).rearrange("p (t n) -> p t n", t=TT)
        cum, ncum = (place(S)[0:FOX_H, :] for _ in range(2))
        cqn = place(TT * Q_RANK).rearrange("p (t n) -> p t n", t=TT)
        ckvn = place(TT * KV_RANK).rearrange("p (t n) -> p t n", t=TT)
        cqT = place(2 * S).rearrange("p (k s) -> p k s", k=2)
        ckvT = place(S)
        ss4, rs4 = place(4), place(4)
        junk = place(S)
        mqr, mq, mk = (place(MLA_H * S).rearrange("p (h s) -> p h s", h=MLA_H) for _ in range(3))
        mv = place(TT * MLA_H * MLA_V).rearrange("p (t n) -> p t n", t=TT)
        kr, kc, ks = (place(S)[NOPE:MLA_QK, :] for _ in range(3))
        ones_at = cursor[0]
        ones4 = place(S)[0:FOX_H, :]
        mqt = arena[:, cursor[0]:cursor[0] + MLA_H * S].rearrange("p (h s) -> p h s", h=MLA_H)
        fu, fa, fe, fl = (arena[0:FOX_H, cursor[0] + i * S:cursor[0] + (i + 1) * S] for i in range(4))
        sc = place(3 * SPAN).rearrange("p (b n) -> p b n", b=3)
        pT = place(2 * SPAN).rearrange("p (b n) -> p b n", b=2)
        nmax, rsum, rinv, nl = (place(2 * NU) for _ in range(4))
        o1 = place(TT * DIFF_V).rearrange("p (t n) -> p t n", t=TT)
        ssd, rsd = place(TT * DIFF_H), place(TT * DIFF_H)
        dsqs = mqr.rearrange("p h s -> p (h s)").rearrange("p (u n) -> p u n", n=DIFF_V)
        end_att = cursor[0]

        cursor[0] = first_free
        y = place(2 * 4 * S).rearrange("p (b g m s) -> p b g m s", b=2, g=2, m=2)
        fsil, hT = (place(2 * 2 * S).rearrange("p (b m s) -> p b m s", b=2, m=2) for _ in range(2))
        cursor[0] += -cursor[0] % 8
        hT1, hT2 = (in_place_of(f"hT{i + 1}", arena, cursor[0] + 4 * S * i, [P, 2, 2, S]) for i in range(2))
        place(2 * 4 * S)
        assert cursor[0] <= ones_at

        where2, table2, table2m = second_constants()
        const2 = nc.inline_tensor(table2, "second_constants").ap()
        const2m = nc.inline_tensor(table2m, "second_masks").ap()
        cursor[0] = where1["ident"][0] + P + par_end
        cst2 = place(table2.shape[1])
        masks2 = place(table2m.shape[1] // 4).bitcast(U8)
        par2 = place(NPAR2)
        ones_s = place(S)
        wr = place(KD * EXPERTS).rearrange("p (k n) -> p k n", k=KD)

        def table(name):
            at, n = where2[name]
            return cst2[:, at:at + n]

        mixer_free = cursor[0]

        def heads(t):
            return t.rearrange("p (h s) -> p h s", h=HEADS)

        z = place(2 * HEADS * S)
        kk = place(2 * HEADS * S)
        e_ = place(2 * HEADS * S)
        ng = place(2 * HEADS * S)
        l1 = place(2 * HEADS * S)
        hqT = place(HEADS * S)
        rqk = place(2 * HEADS * S)
        rv = place(TT * WIDTH).rearrange("p (t n) -> p t n", t=TT)
        hi = place(TT * WIDTH).rearrange("p (t n) -> p t n", t=TT)
        RG = place(TT * WIDTH).rearrange("p (t n) -> p t n", t=TT)
        HG = place(TT * WIDTH).rearrange("p (t n) -> p t n", t=TT)
        ssm, rsm = place(TT * HEADS + TT), place(TT * HEADS + TT)
        LK = [e_[:, 0:HEADS * S], l1[:, 0:HEADS * S]]
        LQ = [e_[:, HEADS * S:], l1[:, HEADS * S:]]
        ST = ng.rearrange("p (s t h n) -> p s t h n", s=TT, t=TT, h=HEADS)
        RS = l1.rearrange("p (h s n) -> p h s n", h=HEADS, s=TT)
        gains2 = XN[:, 0, :].rearrange("p (g n) -> p g n", g=2)
        rot_t = XN[:, 1, :].rearrange("p (b h s) -> p b h s", b=2, h=2)
        lb_t = z[:, 1024:1024 + 32]
        msq = e_[:, 0:WIDTH * TT]

        cursor[0] = mixer_free
        aff, slot_of, elog = (place(TT * EXPERTS).rearrange("p (t e) -> p t e", t=TT) for _ in range(3))
        lmax, lsum, linv = (place(TT) for _ in range(3))
        affT, left, sel, csum, slotT, ones16 = (place(S)[0:EXPERTS, :] for _ in range(6))
        top8 = place(4 * 8)[0:EXPERTS, :].rearrange("p (r n) -> p r n", r=4)
        ONE_HOT = place(TT * EXPERTS * CAP).rearrange("p (t n) -> p t n", t=TT)
        GATED = place(TT * EXPERTS * CAP).rearrange("p (t n) -> p t n", t=TT)
        GT = place(N_GROUPS * S).rearrange("p (g s) -> p g s", g=N_GROUPS)
        pick_g = place(TT * P).rearrange("p (t n) -> p t n", t=TT)
        gate_g = place(S)
        XE = place(KD * P).rearrange("p (k n) -> p k n", k=KD)
        sg = place(2 * S).rearrange("p (b n) -> p b n", b=2)
        hid = place(2 * S).rearrange("p (b n) -> p b n", b=2)
        hidT = place(4 * P).rearrange("p (b i n) -> p b i n", b=2, i=2)
        YE = place(D)

        final_gain = XT[:, 0:4, :].rearrange("p k s -> p (k s)")

        s_small = sem("small_loads")
        s_rows = sem("parameter_rows")
        s_tables = sem("first_constants_in")
        s_zero = sem("rows_cleared")
        s_rowsT = sem("rows_turned")
        s_par = sem("parameters_set")
        s_lamd = sem("lambda_dots")
        s_lame = sem("lambda_exps")
        s_set = sem("setup_steps")
        slot_loaded = [sem(f"slot_loaded{i}") for i in range(SLOTS)]
        slot_free = [sem(f"slot_free{i}") for i in range(SLOTS)]
        par_cur = sem("layer_parameters")
        wu_loaded = sem("mla_weights_loaded")
        sumsq = sem("sums_of_squares")
        rms_in = sem("rms_argument")
        rms = sem("rms_ready")
        xn_ready = sem("normalised")
        turned = sem("turned_in_psum")
        xt1_dve = sem("turned_first_parts_by_dve")
        xt1_act = sem("turned_first_parts_by_act")
        xt_rest = sem("turned_second_parts")
        rounded = sem("weights_first_parts")
        rest = sem("weights_second_parts")
        h_whole = sem("hidden_before_the_split")
        h_round = sem("hidden_first_parts")
        xt_dve = sem("turned_by_dve")
        xt_act = sem("turned_by_act")
        proj = sem("projected")
        free_act = sem("bank_emptied_by_act")
        free_dve = sem("bank_emptied_by_dve")
        lat_sq = sem("latent_squares")
        lat_arg = sem("latent_rms_argument")
        lat_rms = sem("latent_rms")
        latT = sem("latents_turned")
        lat_ready = sem("latents_ready")
        fox_step = sem("forget_gate_steps")
        fox_cum = sem("forget_gate_sums")
        mla_mm = sem("mla_products")
        mla_q = sem("mla_queries_copied")
        mla_qc = sem("mla_queries_times_cos")
        mla_turn = sem("mla_queries_turned")
        mla_kv = sem("mla_keys_copied")
        mla_rot = sem("mla_rotations")
        scored = sem("scores_ready")
        biased = sem("scores_biased")
        probs = sem("probabilities_ready")
        p_turned = sem("probabilities_turned")
        p_copied = sem("turned_probabilities_copied")
        mixed = sem("values_mixed")
        inv_l = sem("softmax_sums_inverted")
        out_done = sem("unit_outputs")
        diff_sq = sem("diff_squares")
        diff_rms = sem("diff_rms_steps")
        diff_done = sem("diff_normalised")
        wo_mm = sem("output_projected")
        x_mid = sem("residual_after_mixer")
        up_mm = sem("up_projected")
        tap2 = sem("last_tap")
        tap1 = sem("middle_tap")
        conv = sem("convolved")
        gate_s = sem("gates_silu")
        h_ready = sem("hidden_ready")
        down_mm = sem("down_projected")
        x_out = sem("residual_after_ffn")
        pass_1 = [xt1_dve, xt1_act, xt_rest, rounded, rest, h_whole, h_round, par_cur, wu_loaded, sumsq, rms_in, rms, xn_ready, turned, xt_dve,
                  xt_act, proj, free_act, free_dve, lat_sq, lat_arg, lat_rms, latT,
                  lat_ready, fox_step, fox_cum, mla_mm, mla_q, mla_qc, mla_turn, mla_kv,
                  mla_rot, scored, biased, probs, p_turned, p_copied, mixed, inv_l,
                  out_done, diff_sq, diff_rms, diff_done, wo_mm, x_mid, up_mm, tap2,
                  tap1, conv, gate_s, h_ready, down_mm, x_out]
        arrived = sem("engines_at_end_of_pass")
        go = {e: sem(f"next_pass_{e}") for e in ("pe", "act", "dve")}

        def end_pass(eng, name):
            eng.sem_inc(arrived, 1)
            eng.wait_ge(go[name], 1)
            eng.sem_clear(go[name])

        def clear_pass(pool, sems):
            pool.wait_ge(arrived, len(go))
            for s in [arrived] + sems:
                pool.sem_clear(s)
            for s in go.values():
                pool.sem_inc(s, 1)

        fin_sq = sem("last_norm_sums_of_squares")
        fin_rms = sem("last_norm_rms_steps")
        fin_gain = sem("last_norm_gain_in")
        fin_done = sem("last_norm_done")
        s_out = sem("output_stored")
        const2_in = sem("second_constants_in")
        set2 = sem("second_setup_steps")
        set2a = sem("lower_bound_exps")
        par2_set = sem("second_parameters_set")

        small2 = sem("layer_gains_and_router_in")
        par2_cur = sem("second_layer_parameters")
        proj2 = sem("items_in_psum")
        emp_act = sem("items_emptied_by_act")
        emp_dve = sem("items_emptied_by_dve")
        z_exp = sem("exp_of_minus_abs_z")
        num = sem("forget_numerators")
        num_max = sem("forget_numerators_clamped")
        lns = sem("forget_logarithms")
        key_r = sem("key_denominators")
        keys = sem("hgrn_keys")
        zmin = sem("deep_forget_terms")
        logf = sem("log_forgets")
        csums = sem("log_forget_sums")
        hq_scaled = sem("hgrn_queries_scaled")
        sub_dve = sem("level_exponents_by_dve")
        sub_pool = sem("level_exponents_by_pool")
        lev_exp = sem("level_exponentials")
        mul_dve = sem("level_queries")
        mul_pool = sem("level_keys")
        lev_mm = sem("level_scores")
        merged = sem("level_scores_merged")
        rot_cos = sem("rotary_cosine_parts")
        rot_sin = sem("rotary_sine_parts")
        rotated = sem("rotated")
        gated = sem("output_gates_ready")
        h_mixed = sem("hgrn_values_mixed")
        r_mixed = sem("retention_values_mixed")
        mix_sq = sem("mixer_squares")
        mix_arg = sem("mixer_rms_argument")
        mix_rms = sem("mixer_rms")
        mix_done = sem("mixer_outputs_ready")
        logits = sem("router_logits")
        soft = sem("router_softmax_steps")
        lexp = sem("router_exponentials")
        affT_mm = sem("affinities_turned")
        top = sem("top_tokens_steps")
        slot_mm = sem("slots_turned")
        hot = sem("one_hot_rows")
        gated_hot = sem("gated_one_hot_rows")
        gt_mm = sem("gates_turned")
        gt_ready = sem("gates_ready")
        pass_2 = [sumsq, rms_in, rms, xn_ready, turned, xt_dve, xt_act, wo_mm, x_mid,
                  small2, par2_cur, proj2, emp_act, emp_dve, z_exp, num, num_max, lns, key_r, keys, zmin, logf,
                  csums, hq_scaled, sub_dve, sub_pool, lev_exp, mul_dve, mul_pool, lev_mm, merged, rot_cos, rot_sin,
                  rotated, gated, h_mixed, r_mixed, mix_sq, mix_arg, mix_rms, mix_done, logits, soft, lexp,
                  affT_mm, top, slot_mm, hot, gated_hot, gt_mm, gt_ready]
        g_sel = sem("group_one_hot_and_gates")
        xe_mm = sem("expert_rows_gathered")
        xe_ready = sem("expert_rows_ready")
        gu_mm = sem("gate_and_up_products")
        g_silu = sem("expert_gates_silu")
        g_hid = sem("expert_hidden")
        hidT_mm = sem("expert_hidden_turned")
        hidT_ready = sem("expert_hidden_turned_ready")
        dn_mm = sem("expert_down_products")
        ye_ready = sem("expert_outputs_ready")
        sc_mm = sem("expert_outputs_scattered")
        x_moe = sem("residual_with_group")
        pass_g = [g_sel, xe_mm, xe_ready, gu_mm, g_silu, g_hid, hidT_mm, hidT_ready, dn_mm, ye_ready, sc_mm, x_moe]

        SMALL, ROWS = 16 * 2, 16 * 17

        def norm_act(act, lay, n, ready):
            for t in range(TT):
                if t == 0:
                    act.wait_ge(*ready)
                nc.scalar.activation(XN[:, t], X[:, t], ACT.Square,
                                     accum_out=ss[:, t:t + 1]).then_inc(sumsq, 1)

        def norm_pool(pool, lay, n):
            pool.wait_ge(sumsq, TT * (n + 1))
            pool.tensor_scalar(rs, ss, 1.0 / D, EPS, ALU.mult, ALU.add).then_inc(rms_in, 1)
            pool.wait_ge(rms_in, n + 1)
            pool.tensor_tensor(rs, rs, expo[:, 0:TT], ALU.pow).then_inc(rms, 1)

        def norm_dve(dve, lay, n):
            dve.wait_ge(rms, n + 1)
            for t in range(TT):
                nc.vector.tensor_scalar(XN[:, t], X[:, t], rs[:, t:t + 1], None,
                                        ALU.mult).then_inc(xn_ready, 1)

        def turn_pe(pe, lay, n):
            for b in range(4):
                for i in range(2):
                    for t in range(TT):
                        last = nc.tensor.transpose(psum[:, b, (2 * i + t) * P:(2 * i + t + 1) * P],
                                                   XN[:, t, (2 * b + i) * P:(2 * b + i + 1) * P], ident)
                last.then_inc(turned, 1)

        def turn_dve(dve, lay, n, gain):
            for b in (0, 2):
                dve.wait_ge(turned, 4 * n + b + 1)
                src = psum[:, b, :].rearrange("p (k s) -> p k s", k=2)
                if gain is None:
                    ins = nc.vector.tensor_copy(XT[:, 2 * b:2 * b + 2, :], src)
                else:
                    ins = nc.vector.tensor_tensor(XT[:, 2 * b:2 * b + 2, :], src,
                                                  gain[:, 2 * b:2 * b + 2].unsqueeze(2).broadcast_to([P, 2, S]),
                                                  ALU.mult)
                ins.then_inc(xt_dve, 1)

        def turn_act(act, lay, n, gain):
            for b in (1, 3):
                act.wait_ge(turned, 4 * n + b + 1)
                for i in range(2):
                    src = psum[:, b, i * S:(i + 1) * S]
                    k = 2 * b + i
                    last = nc.scalar.activation(XT[:, k, :], src, ACT.Copy,
                                                scale=1.0 if gain is None else gain[:, k:k + 1])
                last.then_inc(xt_act, 1)

        def turn_split_act(act, n, gain):
            for k in range(2, KD):
                act.wait_ge(turned, 4 * n + k // 2 + 1)
                nc.scalar.activation(XT1[:, k, :], psum[:, k // 2, (k % 2) * S:(k % 2 + 1) * S], ACT.Copy,
                                     scale=gain[:, k:k + 1]).then_inc(xt1_act, 1)

        def turn_split_dve(dve, n, gain):
            dve.wait_ge(turned, 4 * n + 1)
            for k in range(2):
                nc.vector.tensor_scalar(XT1[:, k, :], psum[:, 0, k * S:(k + 1) * S], gain[:, k:k + 1], None,
                                        ALU.mult).then_inc(xt1_dve, 1)
            for k in range(KD):
                if k < 2:
                    dve.wait_ge(xt1_dve, k + 1)
                else:
                    dve.wait_ge(xt1_act, k // 2 * 2)
                nc.vector.scalar_tensor_tensor(out=XT2[:, k, :], in0=psum[:, k // 2, (k % 2) * S:(k % 2 + 1) * S],
                                               scalar=gain[:, k:k + 1], in1=XT1[:, k, :].bitcast(F32),
                                               op0=ALU.mult, op1=ALU.subtract).then_inc(xt_rest, 1)

        def over(v):
            j, what = ff_use(v)
            return (down_mm, j + 1) if what == 2 else (up_mm, 2 * j + what + 1)

        def split_round(act, v):
            s = v % SLOTS_1
            act.wait_ge(slot_loaded[s], 16)
            act.sem_clear(slot_loaded[s])
            if v >= FF_USE + W_BUFS:
                act.wait_ge(*over(v - W_BUFS))
            elif v == FF_USE + 2:
                act.wait_ge(turned, 4 * 3)
            nc.scalar.activation(W1[(v - FF_USE) % W_BUFS][:, :], slot(s), ACT.Copy).then_inc(rounded, 1)

        def split_rest(dve, v):
            dve.wait_ge(rounded, v - FF_USE + 1)
            nc.vector.tensor_tensor(W2[(v - FF_USE) % W_BUFS][:, :], slot(v % SLOTS_1), W1[(v - FF_USE) % W_BUFS][:, :].bitcast(F32),
                                    ALU.subtract).then_inc(rest, 1)

        def turned_wait(eng, lay, n):
            eng.wait_ge(xt_dve, 2 * (n + 1))
            eng.wait_ge(xt_act, 2 * (n + 1))

        block = ctx.enter_context(nc.Block())

        @block.sync
        def _(sp):
            sp.dma_start(X[:, :, :], w["x"].rearrange("b (t p) d -> p (b t) d", p=P)).then_inc(s_small, 16)
            sp.dma_start(ident, const1[:, 0:P]).then_inc(s_small, 16)

            def columns(dram, lay, c0, n):
                return dram[lay].rearrange("(k p) n -> p k n", p=P)[:, :, c0:c0 + n]

            def claim(s):
                sp.wait_ge(slot_free[s], 1)
                sp.sem_clear(slot_free[s])

            def load(u, lay, src, n, slots=SLOTS_1):
                s = u % slots
                dst = slot(s, 8 * n).rearrange("p (k n) -> p k n", k=8)
                claim(s)
                sp.dma_start(dst, src).then_inc(slot_loaded[s], 16)

            sp.wait_ge(s_rows, ROWS)
            with sp.Fori(0, DEPTH) as lay:
                u = 0
                for name, c0, n in IN_BLOCKS:
                    load(u, lay, columns(w["w_in"], lay, c0, n), n)
                    u += 1
                for i in range(4):
                    load(u, lay, columns(w["w_o"], lay, 256 * i, 256), 256)
                    u += 1
                for v in range(FF_USE, USES_1):
                    j, what = ff_use(v)
                    if what < 2:
                        load(v, lay, columns(w["w_up"], lay, D_FF * what + 256 * j, 256), 256)
                    else:
                        claim(v % SLOTS_1)
                        src = w["w_down"][lay].rearrange("(c k p) n -> c p k n", p=P, k=2)[j]
                        sp.dma_start(slot(v % SLOTS_1).rearrange("p (k n) -> p k n", k=2),
                                     src).then_inc(slot_loaded[v % SLOTS_1], 16)

            with sp.Fori(0, DEPTH) as lay:
                u = 0
                for _, c0 in IN2_BLOCKS:
                    load(u, lay, columns(w["w_in_2"], lay, c0, 256), 256, SLOTS)
                    u += 1
                for i in range(4):
                    load(u, lay, columns(w["w_out_2"], lay, 256 * i, 256), 256, SLOTS)
                    u += 1

                def grouped(name):
                    return w[name][lay].rearrange("(g e) a b -> g e a b", e=GROUP)

                with sp.Fori(0, N_GROUPS) as g:
                    for n in range(F_STEPS):
                        for e in range(GROUP):
                            for i, name in enumerate(("w_gate_2", "w_up_2")):
                                claim(2 * e + i)
                                src = grouped(name)[g][e].rearrange("(k p) f -> p k f", p=P)[:, :, 256 * n:256 * (n + 1)]
                                sp.dma_start(slot(2 * e + i).rearrange("p (k f) -> p k f", k=KD),
                                             src).then_inc(slot_loaded[2 * e + i], 16)
                        for e in range(GROUP):
                            claim(2 * GROUP + e)
                            src = grouped("w_down_2")[g][e].rearrange("(n i p) d -> n p i d", p=P, i=2)[n]
                            sp.dma_start(slot(2 * GROUP + e).rearrange("p (i d) -> p i d", i=2),
                                         src).then_inc(slot_loaded[2 * GROUP + e], 16)

        @block.gpsimd
        def _(pool):
            nc.gpsimd.memset(rows, 0.0).then_inc(s_zero, 1)
            nc.gpsimd.memset(expo10, -0.5).then_inc(s_zero, 1)
            nc.gpsimd.memset(one, 1.0).then_inc(s_zero, 1)
            nc.gpsimd.memset(ones4, 1.0).then_inc(s_zero, 1)
            pool.wait_ge(s_zero, 4)
            with pool.Fori(0, DEPTH) as lay:
                norm_pool(pool, lay, 0)
                pool.wait_ge(lat_sq, 4)
                pool.tensor_scalar(rs4[:, 0:2], ss4[:, 0:2], 1.0 / Q_RANK, EPS, ALU.mult, ALU.add).then_inc(lat_arg, 1)
                pool.tensor_scalar(rs4[:, 2:4], ss4[:, 2:4], 1.0 / KV_RANK, EPS, ALU.mult, ALU.add).then_inc(lat_arg, 1)
                pool.wait_ge(lat_arg, 2)
                pool.tensor_tensor(rs4, rs4, expo[:, 0:4], ALU.pow).then_inc(lat_rms, 1)
                pool.wait_ge(s_tables, 16)
                pool.wait_ge(mla_q, 2)
                pool.tensor_tensor(mq[0:MLA_QK], mqr[0:MLA_QK],
                                   const("cos", MLA_QK).unsqueeze(1).broadcast_to([MLA_QK, MLA_H, S]),
                                   ALU.mult).then_inc(mla_qc, 1)
                pool.wait_ge(diff_sq, 1)
                pool.tensor_scalar(rsd, ssd, 1.0 / DIFF_V, EPS, ALU.mult, ALU.add).then_inc(diff_rms, 1)
                pool.wait_ge(diff_rms, 1)
                pool.tensor_tensor(rsd, rsd, expo[:, 0:TT * DIFF_H], ALU.pow).then_inc(diff_rms, 1)
                heads = XN[:, :, MIX_COL["diff"]:MIX_COL["diff"] + DIFF_H * DIFF_V]
                pool.wait_ge(diff_rms, 2)
                for t in range(TT):
                    hv = heads[:, t].rearrange("p (h n) -> p h n", h=DIFF_H)
                    last = pool.tensor_tensor(hv, hv, rsd[:, t * DIFF_H:(t + 1) * DIFF_H].unsqueeze(2)
                                              .broadcast_to([P, DIFF_H, DIFF_V]), ALU.mult)
                last.then_inc(diff_rms, 1)
                pool.wait_ge(diff_rms, 3)
                for t in range(TT):
                    hv = heads[:, t].rearrange("p (h n) -> p h n", h=DIFF_H)
                    last = pool.tensor_tensor(hv, hv, par[:, C_DG:C_DG + DIFF_V].unsqueeze(1)
                                              .broadcast_to([P, DIFF_H, DIFF_V]), ALU.mult)
                last.then_inc(diff_done, 1)
                norm_pool(pool, lay, 1)
                clear_pass(pool, pass_1)
            pool.wait_ge(fin_sq, TT)
            pool.tensor_scalar(rs, ss, 1.0 / D, EPS, ALU.mult, ALU.add).then_inc(fin_rms, 1)
            pool.wait_ge(fin_rms, 1)
            pool.tensor_tensor(rs, rs, expo[:, 0:TT], ALU.pow).then_inc(fin_rms, 1)

            with pool.Fori(0, DEPTH) as lay:
                norm_pool(pool, lay, 0)
                pool.wait_ge(num, 8)
                pool.tensor_scalar(ng, ng, TINY, None, ALU.max).then_inc(num_max, 1)
                pool.wait_ge(emp_act, 6)
                pool.tensor_scalar(hqT, hqT, HD ** -0.5, None, ALU.mult).then_inc(hq_scaled, 1)

                def sides(t, h):
                    v = t.rearrange("p (n two i) -> p n two i", two=2, i=h)
                    return v[:, :, 0, :], v[:, :, 1, :]

                def exponents(l):
                    h = HALVES[l]
                    dl, dr = sides(z[:, HEADS * S:], h)
                    mid = dr[:, :, 0:1].broadcast_to(list(dl.shape))
                    if l == 0:
                        pool.wait_ge(csums, 2 * HEADS + 1)
                        pool.wait_ge(keys, 8)
                    if l >= 2:
                        pool.wait_ge(lev_mm, l - 1)
                    pool.tensor_tensor(sides(LK[l % 2], h)[1], dr, mid, ALU.subtract)
                    pool.tensor_tensor(sides(LQ[l % 2], h)[0], mid, dl, ALU.subtract).then_inc(sub_pool, 1)

                def level_keys(l):
                    h = HALVES[l]
                    pool.wait_ge(lev_exp, 2 * l + 1)
                    for i in range(2):
                        lk = sides(LK[l % 2], h)[i]
                        last = pool.tensor_tensor(lk, lk, sides(kk[:, i * HEADS * S:(i + 1) * HEADS * S], h)[i], ALU.mult)
                    last.then_inc(mul_pool, 1)

                for l in range(len(HALVES) + 1):
                    if l < len(HALVES):
                        exponents(l)
                    if l >= 1:
                        level_keys(l - 1)
                pool.wait_ge(lev_mm, LEVELS - 2)
                pool.tensor_tensor(LK[0], kk[:, 0:HEADS * S], kk[:, HEADS * S:], ALU.add).then_inc(mul_pool, 1)
                pool.wait_ge(small2, 48)
                for i, (t_, n) in enumerate(((RG, 16), (HG, 18))):
                    pool.wait_ge(emp_act, n)
                    pool.tensor_tensor(t_[:, :, :], t_[:, :, :],
                                       gains2[:, i, :].unsqueeze(1).broadcast_to([P, TT, WIDTH]), ALU.mult).then_inc(gated, 1)
                pool.wait_ge(mix_sq, TT * HEADS + TT)
                pool.tensor_scalar(rsm[:, 0:TT * HEADS], ssm[:, 0:TT * HEADS], 1.0 / HD, EPS, ALU.mult, ALU.add).then_inc(mix_arg, 1)
                pool.tensor_scalar(rsm[:, TT * HEADS:], ssm[:, TT * HEADS:], 1.0 / WIDTH, EPS, ALU.mult, ALU.add).then_inc(mix_arg, 1)
                pool.wait_ge(mix_arg, 2)
                pool.tensor_tensor(rsm, rsm, expo10, ALU.pow).then_inc(mix_rms, 1)
                norm_pool(pool, lay, 1)
                pool.wait_ge(hot, TT)
                for t in range(TT):
                    pool.tensor_tensor(GATED[:, t].rearrange("p (e c) -> p e c", c=CAP),
                                       ONE_HOT[:, t].rearrange("p (e c) -> p e c", c=CAP),
                                       aff[:, t].unsqueeze(2).broadcast_to([P, EXPERTS, CAP]),
                                       ALU.mult).then_inc(gated_hot, 1)
                pool.wait_ge(gt_ready, 2)

                with pool.Fori(0, N_GROUPS) as g:
                    pool.tensor_copy(pick_g[:, :, :], ONE_HOT.rearrange("p t (g n) -> p t g n", g=N_GROUPS)[:, :, g, :]).then_inc(g_sel, 1)
                    pool.tensor_copy(gate_g, GT[:, g, :]).then_inc(g_sel, 1)
                    clear_pass(pool, pass_g)
                clear_pass(pool, pass_2)

            pool.wait_ge(fin_sq, TT + TT)
            pool.tensor_scalar(rs, ss, 1.0 / D, EPS, ALU.mult, ALU.add).then_inc(fin_rms, 1)
            pool.wait_ge(fin_rms, 2 + 1)
            pool.tensor_tensor(rs, rs, expo[:, 0:TT], ALU.pow).then_inc(fin_rms, 1)

        @block.scalar
        def _(act):
            act.wait_ge(s_zero, 4)
            taps = [w["conv_w"][:, j, :].rearrange("l (r p) -> r l p", p=P) for j in range(3)]
            vec = lambda name: w[name].rearrange("l (r p) -> r l p", p=P)
            wide = lambda name, n: w[name].unsqueeze(0).broadcast_to([P, DEPTH, n])
            for dst, src in [
                (rows[C_LN1:C_LN1 + 8, :, 0, :], vec("ln1_g")), (rows[0:44, :, 0, :], taps[0]),
                (rows[44:88, :, 0, :], taps[1]), (rows[C_LN2:C_LN2 + 8, :, 0, :], vec("ln2_g")),
                (rows[C_QN:C_QN + 2, :, 0, :], vec("q_norm_g")), (rows[C_KVN:C_KVN + 1, :, 0, :], vec("kv_norm_g")),
                (rows[C_FG:C_FG + 1, :, 0, 0:FOX_H], w["fgate_b"].unsqueeze(0)),
                (rows[0:44, :, 1, :], taps[2]), (rows[44:88, :, 1, :], vec("conv_b")),
                (rows[88:96, :, 1, :], vec("norm1_g_2")), (rows[96:104, :, 1, :], vec("norm2_g_2")),
                (rows[104:108, :, 1, :], vec("lower_bounds_2")),
                (par_all[:, :, C_DG:C_DG + DIFF_V], wide("diff_norm_g", DIFF_V)),
                (lamv[:, :, 0, :], wide("lam_q1", DIFF_QK)), (lamv[:, :, 1, :], wide("lam_k1", DIFF_QK)),
                (lamv[:, :, 2, :], wide("lam_q2", DIFF_QK)), (lamv[:, :, 3, :], wide("lam_k2", DIFF_QK)),
            ]:
                act.dma_start(dst, src).then_inc(s_rows, 16)
            act.wait_ge(s_lamd, 2 * DEPTH)
            act.dma_start(cst[:, P:], const1[:, P:]).then_inc(s_tables, 16)
            nc.scalar.activation(lame, lams, ACT.Exp).then_inc(s_lame, 1)
            with act.Fori(0, DEPTH) as lay:
                act.wait_ge(par_cur, 1)
                act.dma_start(wf, w["w_in"][lay].rearrange("(k p) n -> p k n", p=P)[:, :, 768:772]).then_inc(wu_loaded, 16)
                act.dma_start(wuq, w["w_uq"][lay].rearrange("(k p) n -> p k n", p=P)).then_inc(wu_loaded, 16)
                act.dma_start(wukv, w["w_ukv"][lay]).then_inc(wu_loaded, 16)
                norm_act(act, lay, 0, (par_cur, 1))
                turn_act(act, lay, 0, par[:, C_LN1:C_LN1 + 8])

                def block_out(i):
                    return psum[:, 4 + i % 4, :]

                act.wait_ge(proj, 1)
                for t in range(TT):
                    if t:
                        act.wait_ge(lat_sq, t)
                    nc.scalar.activation(junk, block_out(0)[:, t * S:(t + 1) * S], ACT.Square,
                                         accum_out=ss4[:, t:t + 1]).then_inc(lat_sq, 1)
                act.wait_ge(proj, 2)
                for t in range(TT):
                    act.wait_ge(lat_sq, 2 + t)
                    nc.scalar.activation(junk[:, 0:KV_RANK], block_out(1)[:, t * KV_RANK:(t + 1) * KV_RANK], ACT.Square,
                                         accum_out=ss4[:, 2 + t:3 + t]).then_inc(lat_sq, 1)
                act.wait_ge(proj, 4)
                nc.scalar.activation(fu, psum[0:FOX_H, 0, 0:S], ACT.Identity,
                                     bias=par[0:FOX_H, C_FG:C_FG + 1]).then_inc(fox_step, 1)
                act.wait_ge(fox_step, 1)
                nc.scalar.activation(fa, fu, ACT.Abs).then_inc(fox_step, 1)
                act.wait_ge(fox_step, 2)
                nc.scalar.activation(fe, fa, ACT.Exp, scale=-1.0).then_inc(fox_step, 1)
                act.wait_ge(fox_step, 3)
                nc.scalar.activation(fl, fe, ACT.Ln, bias=one[0:FOX_H, :]).then_inc(fox_step, 1)
                for i, dst, k in ((3, fqT[:, :, :], -FOX_D ** -0.5), (5, dqT[:, 0:2, :], -DIFF_QK ** -0.5),
                                  (6, dqT[:, 2:4, :], -DIFF_QK ** -0.5), (9, dv[:, :, 0:S], 1.0)):
                    act.wait_ge(proj, i + 1 + (i >= 3))
                    nc.scalar.activation(dst, block_out(i).rearrange("p (a b) -> p a b", a=2), ACT.Copy,
                                         scale=k).then_inc(free_act, 1)
                for b in range(2):
                    act.wait_ge(mla_mm, b + 1)
                    nc.scalar.activation(mqr[0:MLA_QK, 2 * b:2 * b + 2, :],
                                         psum[0:MLA_QK, 2 + b, :].rearrange("p (a b) -> p a b", a=2), ACT.Copy,
                                         scale=-MLA_QK ** -0.5).then_inc(mla_q, 1)

                def probabilities(j):
                    act.wait_ge(biased, 2 * (j + 1))
                    for t, (a, b) in enumerate(((0, P), (P, SPAN))):
                        last = nc.scalar.activation(sc[:, j % 3, a:b], sc[:, j % 3, a:b], ACT.Exp, scale=-1.0,
                                                    bias=nmax[:, 2 * j + t:2 * j + t + 1],
                                                    accum_out=rsum[:, 2 * j + t:2 * j + t + 1])
                    last.then_inc(probs, 1)

                def copy_turned(j):
                    act.wait_ge(p_turned, j + 1)
                    nc.scalar.activation(pT[:, j % 2, :], psum[:, 2 + j % 2, 0:SPAN], ACT.Copy).then_inc(p_copied, 1)

                for j in range(NU + 1):
                    if j < NU:
                        probabilities(j)
                    if j >= 1:
                        copy_turned(j - 1)
                    if j == 2 * DIFF_H + 2:
                        act.wait_ge(out_done, 2 * DIFF_H)
                        for t in range(TT):
                            for h in range(DIFF_H):
                                c = MIX_COL["diff"] + h * DIFF_V
                                last = nc.scalar.activation(dsqs[:, t * DIFF_H + h, :], XN[:, t, c:c + DIFF_V], ACT.Square,
                                                            accum_out=ssd[:, t * DIFF_H + h:t * DIFF_H + h + 1])
                        last.then_inc(diff_sq, 1)
                turn_act(act, lay, 1, None)
                split_round(act, FF_USE)
                split_round(act, FF_USE + 1)
                norm_act(act, lay, 1, (x_mid, 4))
                turn_split_act(act, 2, par[:, C_LN2:C_LN2 + 8])
                split_round(act, FF_USE + 2)
                for j in range(FF_STEPS):
                    for g in range(2):
                        act.wait_ge(up_mm, 2 * j + g + 1)
                        if FF_OF[j, g] + W_BUFS < USES_1:
                            split_round(act, FF_OF[j, g] + W_BUFS)
                        if j >= 2 and g == 0:
                            act.wait_ge(h_whole, j - 1)
                        for m in range(2):
                            c = g * FF_CH + 2 * j + m
                            last = nc.scalar.activation(
                                y[:, j % 2, g, m, :], psum[:, 4 + 2 * (j % 2) + g, m * S:(m + 1) * S], ACT.Identity,
                                scale=par[:, C_W2 + c:C_W2 + c + 1], bias=par[:, C_CB + c:C_CB + c + 1])
                        last.then_inc(tap2, 1)
                    act.wait_ge(conv, j + 1)
                    nc.scalar.activation(fsil[:, j % 2], y[:, j % 2, 0], ACT.Silu).then_inc(gate_s, 1)
                    act.wait_ge(h_whole, j + 1)
                    if j >= 2:
                        act.wait_ge(down_mm, j - 1)
                    nc.scalar.activation(hT1[:, j % 2], hT[:, j % 2], ACT.Copy).then_inc(h_round, 1)
                    if j >= 1 and FF_OF[j - 1, 2] + W_BUFS < USES_1:
                        split_round(act, FF_OF[j - 1, 2] + W_BUFS)
                end_pass(act, "act")
            act.dma_start(final_gain, w["final_g"].rearrange("(o d) -> o d", o=1).broadcast_to([P, D])).then_inc(fin_gain, 16)
            for t in range(TT):
                nc.scalar.activation(XN[:, t], X[:, t], ACT.Square, accum_out=ss[:, t:t + 1]).then_inc(fin_sq, 1)

            act.dma_start(cst2, const2).then_inc(const2_in, 16)
            act.dma_start(masks2, const2m).then_inc(const2_in, 16)
            act.wait_ge(set2, 2)
            nc.scalar.activation(lb_t[:, 8:16], lb_t[:, 8:16], ACT.Exp).then_inc(set2a, 1)
            with act.Fori(0, DEPTH) as lay:
                act.wait_ge(par2_cur, 1)
                act.dma_start(wr, w["w_router_2"][lay].rearrange("(k p) n -> p k n", p=P)).then_inc(small2, 16)
                norm_act(act, lay, 0, (par2_cur, 1))
                turn_act(act, lay, 0, par2[:, C2_N1:C2_N1 + 8])
                act.wait_ge(turned, 4)
                for i, name in enumerate(("ret_norm_g_2", "hgrn_norm_g_2")):
                    act.dma_start(gains2[:, i, :], w[name][bass.ds(lay, 1), :].broadcast_to([P, WIDTH])).then_inc(small2, 16)

                def two(dst):
                    return dst.rearrange("p (a b) -> p a b", a=2)

                def empty(n):
                    i = ITEMS[n][1]
                    name = IN2_BLOCKS[i][0]
                    half = int(name[2])
                    src = psum[:, 4 + n % 4, :]
                    act.wait_ge(proj2, n + 1)
                    if name[:2] in ("zf", "zb"):
                        c = (name[:2] == "zb") * HEADS * S + half * 512
                        nc.scalar.activation(z[:, c:c + 512], src, ACT.Copy)
                        nc.scalar.activation(e_[:, c:c + 512], src, ACT.Abs).then_inc(emp_act, 1)
                        act.wait_ge(emp_act, n + 1)
                        nc.scalar.activation(e_[:, c:c + 512], e_[:, c:c + 512], ACT.Exp, scale=-1.0).then_inc(z_exp, 1)
                        return
                    c = 512 * half
                    if name[:2] == "hq":
                        dst, f = hqT[:, c:c + 512], ACT.Silu
                    elif name[:2] in ("rq", "rk"):
                        c += (name[:2] == "rk") * HEADS * S
                        dst, f = rqk[:, c:c + 512], ACT.Copy
                    else:
                        buf, f = {"rv": (rv, ACT.Copy), "hi": (hi, ACT.Copy), "rg": (RG, ACT.Silu), "hg": (HG, ACT.Silu)}[name[:2]]
                        dst, src = buf[:, :, 256 * half:256 * (half + 1)], two(src)
                    nc.scalar.activation(dst, src, f).then_inc(emp_act, 1)

                def level_exp(l):
                    act.wait_ge(sub_dve, l + 1)
                    act.wait_ge(sub_pool, l + 1)
                    nc.scalar.activation(LK[l % 2], LK[l % 2], ACT.Exp).then_inc(lev_exp, 1)
                    nc.scalar.activation(LQ[l % 2], LQ[l % 2], ACT.Exp).then_inc(lev_exp, 1)

                for n in range(6):
                    empty(n)
                act.wait_ge(z_exp, 4)
                nc.scalar.activation(l1, e_, ACT.Ln, bias=one).then_inc(lns, 1)
                act.wait_ge(num_max, 1)
                nc.scalar.activation(ng, ng, ACT.Ln).then_inc(lns, 1)
                for n in range(6, 10):
                    empty(n)
                level_exp(0)
                level_exp(1)
                for n in range(14, 22):
                    empty(n)
                    if n - 12 < len(HALVES):
                        level_exp(n - 12)
                for t in range(TT):
                    act.wait_ge(h_mixed, t + 1)
                    if t == 0:
                        act.wait_ge(merged, LEVELS)
                    nc.scalar.activation(msq[:, t * WIDTH:(t + 1) * WIDTH], psum[:, t, :], ACT.Square,
                                         accum_out=ssm[:, TT * HEADS + t:TT * HEADS + t + 1]).then_inc(mix_sq, 1)
                for t in range(TT):
                    act.wait_ge(r_mixed, t + 1)
                    if t == 0:
                        act.wait_ge(mix_sq, TT)
                    for h in range(HEADS):
                        nc.scalar.activation(msq[:, t * WIDTH + h * HD:t * WIDTH + (h + 1) * HD],
                                             psum[:, 2 + t, h * HD:(h + 1) * HD], ACT.Square,
                                             accum_out=ssm[:, t * HEADS + h:t * HEADS + h + 1]).then_inc(mix_sq, 1)
                turn_act(act, lay, 1, None)
                norm_act(act, lay, 1, (x_mid, 4))
                turn_act(act, lay, 2, par2[:, C2_N2:C2_N2 + 8])
                act.wait_ge(soft, 2)
                for t in range(TT):
                    last = nc.scalar.activation(elog[:, t], psum[:, 4, t * EXPERTS:(t + 1) * EXPERTS], ACT.Exp,
                                                bias=lmax[:, t:t + 1], accum_out=lsum[:, t:t + 1])
                last.then_inc(lexp, 1)
                for b in range(2):
                    act.wait_ge(gt_mm, b + 1)
                    nc.scalar.activation(GT[:, 2 * b:2 * b + 2, :], psum[:, 6 + b, :].rearrange("p (g s) -> p g s", g=2),
                                         ACT.Copy).then_inc(gt_ready, 1)

                with act.Fori(0, N_GROUPS) as g:
                    for n in range(F_STEPS):
                        act.wait_ge(gu_mm, n + 1)
                        if n >= 2:
                            act.wait_ge(g_hid, n - 1)
                        nc.scalar.activation(sg[:, n % 2], psum[:, 2 + n % 2, 0:256], ACT.Silu).then_inc(g_silu, 1)
                        act.wait_ge(hidT_mm, n + 1)
                        if n >= 2:
                            act.wait_ge(dn_mm, n - 1)
                        nc.scalar.activation(hidT[:, n % 2], psum[:, 4 + n % 2, 0:256].rearrange("p (i n) -> p i n", i=2),
                                             ACT.Copy).then_inc(hidT_ready, 1)
                    act.wait_ge(dn_mm, F_STEPS)
                    nc.scalar.activation(YE[:, 0:512], psum[:, 6, :], ACT.Copy).then_inc(ye_ready, 1)
                    end_pass(act, "act")
                end_pass(act, "act")
            for t in range(TT):
                nc.scalar.activation(XN[:, t], X[:, t], ACT.Square, accum_out=ss[:, t:t + 1]).then_inc(fin_sq, 1)
            act.dma_start(final_gain, w["final_norm_g_2"].rearrange("(o d) -> o d", o=1).broadcast_to([P, D])).then_inc(fin_gain, 16)
            for t in range(TT):
                act.wait_ge(fin_done, TT + t + 1)
                act.dma_start(out[0, t * P:(t + 1) * P, :], X[:, t, :]).then_inc(s_out, 16)
            act.wait_ge(s_out, 16 * TT)

        @block.vector
        def _(dve):
            dve.wait_ge(s_small, SMALL)
            dve.wait_ge(s_rows, ROWS)
            for l in range(DEPTH):
                for i in range(2):
                    if l or i:
                        dve.wait_ge(s_lamd, 2 * l + i)
                    nc.vector.tensor_tensor_reduce(lamp, lamv[:, l, 2 * i, :], lamv[:, l, 2 * i + 1, :], 1.0, 0.0,
                                                   ALU.mult, ALU.add, lams[:, 2 * l + i:2 * l + i + 1]).then_inc(s_lamd, 1)
            for l in range(DEPTH):
                init = 0.8 - 0.6 * math.exp(-0.3 * l)
                nc.vector.tensor_scalar(par_all[:, l, C_DG:C_DG + DIFF_V], par_all[:, l, C_DG:C_DG + DIFF_V],
                                        1.0 - init, None, ALU.mult).then_inc(s_par, 1)
                for i in range(2):
                    dve.wait_ge(s_rowsT, 2 * l + i + 1)
                    nc.vector.tensor_copy(par_all[:, l, P * i:P * i + P],
                                          psum[:, 2 * l + i, 0:P]).then_inc(s_par, 1)
                if l == 0:
                    dve.wait_ge(s_lame, 1)
                nc.vector.tensor_tensor(par_all[:, l, C_NLAM:C_NLAM + 1], lame[:, 2 * l + 1:2 * l + 2],
                                        lame[:, 2 * l:2 * l + 1], ALU.subtract).then_inc(s_set, 1)
                dve.wait_ge(s_set, l + 1)
                nc.vector.tensor_scalar(par_all[:, l, C_NLAM:C_NLAM + 1], par_all[:, l, C_NLAM:C_NLAM + 1],
                                        -init, None, ALU.add).then_inc(s_par, 1)
            dve.wait_ge(s_par, 4 * DEPTH)
            for l in range(DEPTH):
                nc.vector.tensor_copy(par2_all[:, l, 0:20], par_all[:, l, C_SECOND:C_SECOND + 20]).then_inc(par2_set, 1)

            with dve.Fori(0, DEPTH) as lay:
                nc.vector.tensor_copy(par, par_all[:, lay, :]).then_inc(par_cur, 1)
                dve.wait_ge(par_cur, 1)
                norm_dve(dve, lay, 0)
                turn_dve(dve, lay, 0, par[:, C_LN1:C_LN1 + 8])

                def bank(i):
                    return psum[:, 4 + i % 4, :]

                def projected(i):
                    dve.wait_ge(proj, i + 1 + (i >= 3))

                dve.wait_ge(lat_rms, 1)
                for t in range(TT):
                    last = nc.vector.tensor_scalar(cqn[:, t], bank(0)[:, t * S:(t + 1) * S], rs4[:, t:t + 1], None, ALU.mult)
                last.then_inc(free_dve, 1)
                for t in range(TT):
                    nc.vector.tensor_scalar(ckvn[:, t], bank(1)[:, t * KV_RANK:(t + 1) * KV_RANK],
                                            rs4[:, 2 + t:3 + t], None, ALU.mult)
                nc.vector.tensor_copy(kr, psum[NOPE:MLA_QK, 5, S:2 * S]).then_inc(free_dve, 1)
                projected(2)
                nc.vector.tensor_copy(fv[:, :, :], bank(2).rearrange("p (t n) -> p t n", t=TT)).then_inc(free_dve, 1)
                dve.wait_ge(fox_step, 4)
                nc.vector.scalar_tensor_tensor(out=fa, in0=fu, scalar=0.0, in1=fl, op0=ALU.min,
                                               op1=ALU.subtract).then_inc(fox_cum, 1)
                dve.wait_ge(fox_cum, 1)
                nc.vector.tensor_tensor_scan(cum, ones4, fa, 0.0, ALU.mult, ALU.add).then_inc(fox_cum, 1)
                dve.wait_ge(fox_cum, 2)
                nc.vector.tensor_scalar(ncum, cum, -1.0, None, ALU.mult).then_inc(fox_cum, 1)
                projected(4)
                nc.vector.tensor_copy(fkT[:, :, :], bank(4).rearrange("p (m s) -> p m s", m=2)).then_inc(free_dve, 1)
                dve.wait_ge(latT, 1)
                nc.vector.tensor_tensor(cqT[:, :, :], psum[:, 0, :].rearrange("p (k s) -> p k s", k=2),
                                        par[:, C_QN:C_QN + 2].unsqueeze(2).broadcast_to([P, 2, S]),
                                        ALU.mult).then_inc(lat_ready, 1)
                dve.wait_ge(latT, 2)
                nc.vector.tensor_scalar(ckvT, psum[:, 1, 0:S], par[:, C_KVN:C_KVN + 1], None,
                                        ALU.mult).then_inc(lat_ready, 1)
                for i, dst in ((7, dkT[:, 0:2, :]), (8, dkT[:, 2:4, :]), (10, dv[:, :, S:2 * S])):
                    projected(i)
                    nc.vector.tensor_copy(dst, bank(i).rearrange("p (a b) -> p a b", a=2)).then_inc(free_dve, 1)
                for b in range(2):
                    dve.wait_ge(mla_mm, 3 + b)
                    nc.vector.tensor_copy(mk[0:NOPE, 2 * b:2 * b + 2, :],
                                          psum[0:NOPE, b, :].rearrange("p (h s) -> p h s", h=2)).then_inc(mla_kv, 1)
                dve.wait_ge(mla_mm, 5)
                nc.vector.tensor_copy(mv[:, :, :], psum[:, 4, :].rearrange("p (t n) -> p t n", t=TT)).then_inc(mla_kv, 1)
                dve.wait_ge(s_tables, 16)
                nc.vector.tensor_tensor(kc, kr, cst[NOPE:MLA_QK, where1["cos"][0]:where1["cos"][0] + S],
                                        ALU.mult).then_inc(mla_rot, 1)
                dve.wait_ge(mla_mm, 6)
                nc.vector.tensor_tensor(ks, psum[NOPE:MLA_QK, 5, 0:S], cst[NOPE:MLA_QK, where1["sin"][0]:where1["sin"][0] + S],
                                        ALU.mult).then_inc(mla_rot, 1)
                dve.wait_ge(mla_rot, 2)
                nc.vector.tensor_tensor(mk[NOPE:MLA_QK, :, :], kc.unsqueeze(1).broadcast_to([ROPE, MLA_H, S]),
                                        ks.unsqueeze(1).broadcast_to([ROPE, MLA_H, S]), ALU.add).then_inc(mla_rot, 1)
                for b in range(2):
                    dve.wait_ge(mla_turn, b + 1)
                    last = nc.vector.tensor_tensor(mqt[0:MLA_QK, 2 * b:2 * b + 2, :],
                                                   psum[0:MLA_QK, 6 + b, :].rearrange("p (h s) -> p h s", h=2),
                                                   const("sin", MLA_QK).unsqueeze(1).broadcast_to([MLA_QK, 2, S]), ALU.mult)
                    last.then_inc(mla_rot, 1)
                dve.wait_ge(mla_rot, 5)
                dve.wait_ge(mla_qc, 1)
                nc.vector.tensor_tensor(mq[0:MLA_QK], mq[0:MLA_QK], mqt[0:MLA_QK], ALU.add).then_inc(mla_rot, 1)

                dve.wait_ge(mla_rot, 6)
                n_inv = [0]

                def bias_and_max(j):
                    g, h, i = UNITS[j]
                    table = {"fox": "fox_mask", "mla": "mla_mask", "diff": f"diff_mask{h}"}[g]
                    dve.wait_ge(scored, j + 1)
                    for t, (a, b) in enumerate(((0, P), (P, SPAN))):
                        nc.vector.tensor_tensor_reduce(sc[:, j % 3, a:b], psum[:, j % 2, a:b], const(table)[:, a:b],
                                                       1.0, 3.0e38, ALU.add, ALU.min,
                                                       nmax[:, 2 * j + t:2 * j + t + 1]).then_inc(biased, 1)

                def outputs(j):
                    g, h, i = UNITS[j]
                    n = DIFF_V if g == "diff" else 64
                    src = psum[:, 4 + j % 2, 0:TT * n].rearrange("p (t n) -> p t n", t=TT)
                    c = MIX_COL[g] + h * n
                    dst = XN[:, :, c:c + n]
                    r = rinv[:, 2 * j:2 * j + 2]
                    dve.wait_ge(mixed, j + 1)
                    nc.vector.reciprocal(r, rsum[:, 2 * j:2 * j + 2]).then_inc(inv_l, 1)
                    n_inv[0] += 1
                    dve.wait_ge(inv_l, n_inv[0])
                    if g != "diff" or i == 0:
                        nc.vector.tensor_tensor(o1[:, :, :] if g == "diff" else dst, src,
                                                r.unsqueeze(2).broadcast_to([P, TT, n]), ALU.mult).then_inc(out_done, 1)
                        return
                    nc.vector.tensor_scalar(nl[:, 2 * j:2 * j + 2], r, par[:, C_NLAM:C_NLAM + 1], None,
                                            ALU.mult).then_inc(inv_l, 1)
                    n_inv[0] += 1
                    dve.wait_ge(inv_l, n_inv[0])
                    dve.wait_ge(out_done, j)
                    for t in range(TT):
                        last = nc.vector.scalar_tensor_tensor(out=dst[:, t], in0=src[:, t],
                                                              scalar=nl[:, 2 * j + t:2 * j + t + 1],
                                                              in1=o1[:, t], op0=ALU.mult, op1=ALU.add)
                    last.then_inc(out_done, 1)

                for j in range(NU + 2):
                    if j < NU:
                        bias_and_max(j)
                    if j >= 2:
                        outputs(j - 2)
                turn_dve(dve, lay, 1, None)
                for i in range(4):
                    if i < 2:
                        split_rest(dve, FF_USE + i)
                    dve.wait_ge(wo_mm, i + 1)
                    dst = X[:, :, 256 * i:256 * (i + 1)]
                    nc.vector.tensor_tensor(dst, psum[:, 4 + i, :].rearrange("p (t n) -> p t n", t=TT), dst,
                                            ALU.add).then_inc(x_mid, 1)
                dve.wait_ge(x_mid, 4)
                norm_dve(dve, lay, 1)
                turn_split_dve(dve, 2, par[:, C_LN2:C_LN2 + 8])
                split_rest(dve, FF_USE + 2)
                for j in range(FF_STEPS):
                    for g in range(2):
                        if FF_OF[j, g] + W_BUFS < USES_1:
                            split_rest(dve, FF_OF[j, g] + W_BUFS)
                    dve.wait_ge(tap2, 2 * (j + 1))
                    for tap, col, done in ((1, C_W1, tap1), (2, C_W0, conv)):
                        if tap == 2:
                            dve.wait_ge(tap1, j + 1)
                        for g in range(2):
                            for m in range(2):
                                c = g * FF_CH + 2 * j + m
                                dst = y[:, j % 2, g, m, tap:S]
                                last = nc.vector.scalar_tensor_tensor(
                                    out=dst, in0=psum[:, 4 + 2 * (j % 2) + g, m * S:m * S + S - tap],
                                    scalar=par[:, col + c:col + c + 1], in1=dst, op0=ALU.mult, op1=ALU.add)
                        last.then_inc(done, 1)
                    dve.wait_ge(gate_s, j + 1)
                    nc.vector.tensor_tensor(hT[:, j % 2], fsil[:, j % 2], y[:, j % 2, 1], ALU.mult).then_inc(h_whole, 1)
                    if j >= 1 and FF_OF[j - 1, 2] + W_BUFS < USES_1:
                        split_rest(dve, FF_OF[j - 1, 2] + W_BUFS)
                    dve.wait_ge(h_round, j + 1)
                    nc.vector.tensor_tensor(hT2[:, j % 2], hT[:, j % 2], hT1[:, j % 2].bitcast(F32),
                                            ALU.subtract).then_inc(h_ready, 1)
                dve.wait_ge(down_mm, FF_STEPS)
                for t in range(TT):
                    for c in range(2):
                        dst = X[:, t, 512 * c:512 * (c + 1)]
                        nc.vector.tensor_tensor(dst, psum[:, 2 * t + c, :], dst, ALU.add).then_inc(x_out, 1)
                dve.wait_ge(x_out, 4)
                end_pass(dve, "dve")
            dve.wait_ge(par2_set, 2)
            low = [par2_all[:, l, C2_LB:C2_LB + HEADS] for l in range(DEPTH)]
            steps = [1]

            def step(ins):
                ins.then_inc(set2, 1)
                dve.wait_ge(set2, steps[0])
                steps[0] += 1

            step(nc.vector.tensor_tensor(lb_t[:, 0:4], low[0], low[1], ALU.max))
            nc.vector.tensor_tensor(lb_t[:, 8:12], low[0], lb_t[:, 0:4], ALU.subtract)
            step(nc.vector.tensor_tensor(lb_t[:, 12:16], low[1], lb_t[:, 0:4], ALU.subtract))
            dve.wait_ge(set2a, 1)
            step(nc.vector.tensor_tensor(lb_t[:, 16:20], lb_t[:, 8:12], lb_t[:, 12:16], ALU.add))
            step(nc.vector.reciprocal(lb_t[:, 16:20], lb_t[:, 16:20]))
            nc.vector.tensor_tensor(lb_t[:, 8:12], lb_t[:, 8:12], lb_t[:, 16:20], ALU.mult)
            step(nc.vector.tensor_tensor(lb_t[:, 12:16], lb_t[:, 12:16], lb_t[:, 16:20], ALU.mult))
            nc.vector.tensor_tensor(low[0], lb_t[:, 8:12], lb_t[:, 8:12], ALU.subtract)
            step(nc.vector.tensor_tensor(low[1], lb_t[:, 8:12], lb_t[:, 12:16], ALU.add))
            step(nc.vector.tensor_tensor(low[1], low[1], lb_t[:, 8:12], ALU.subtract))
            for l in range(DEPTH):
                nc.vector.tensor_scalar(par2_all[:, l, C2_OML:C2_OML + 4], low[l], -1.0, 1.0, ALU.mult, ALU.add)
                step(nc.vector.tensor_scalar(par2_all[:, l, C2_FLAG:C2_FLAG + 4], low[l], 0.0, None, ALU.is_equal))
            step(nc.vector.memset(ones_s, 1.0))
            dve.wait_ge(fin_rms, 2)
            dve.wait_ge(fin_gain, 16)
            for t in range(TT):
                nc.vector.scalar_tensor_tensor(out=X[:, t], in0=X[:, t], scalar=rs[:, t:t + 1], in1=final_gain,
                                               op0=ALU.mult, op1=ALU.mult).then_inc(fin_done, 1)
            dve.wait_ge(fin_done, TT)

            with dve.Fori(0, DEPTH) as lay:
                nc.vector.tensor_copy(par2, par2_all[:, lay, :]).then_inc(par2_cur, 1)
                dve.wait_ge(par2_cur, 1)
                norm_dve(dve, lay, 0)
                turn_dve(dve, lay, 0, par2[:, C2_N1:C2_N1 + 8])

                def head(t, i):
                    return t[:, i * S:(i + 1) * S]

                for b in range(4):
                    c = slice(512 * b, 512 * (b + 1))
                    dve.wait_ge(z_exp, b + 1)
                    nc.vector.scalar_tensor_tensor(out=kk[:, c], in0=z[:, c], scalar=0.0, in1=e_[:, c], op0=ALU.is_lt, op1=ALU.max)
                    nc.vector.scalar_tensor_tensor(out=ng[:, c], in0=z[:, c], scalar=0.0, in1=e_[:, c], op0=ALU.is_ge,
                                                   op1=ALU.max).then_inc(key_r, 1)
                    dve.wait_ge(key_r, b + 1)
                    for i in (2 * b, 2 * b + 1):
                        nc.vector.scalar_tensor_tensor(out=head(ng, i), in0=head(kk, i), scalar=par2[:, C2_LB + i % 4:C2_LB + i % 4 + 1],
                                                       in1=head(ng, i), op0=ALU.mult, op1=ALU.add).then_inc(num, 1)
                dve.wait_ge(lns, 1)
                nc.vector.tensor_scalar(e_, e_, 1.0, None, ALU.add).then_inc(key_r, 1)
                dve.wait_ge(key_r, 5)
                nc.vector.reciprocal(e_, e_).then_inc(key_r, 1)
                nc.vector.tensor_scalar(z, z, LOG_TINY, 0.0, ALU.add, ALU.min).then_inc(zmin, 1)
                dve.wait_ge(key_r, 6)
                for i in range(8):
                    nc.vector.scalar_tensor_tensor(out=head(kk, i), in0=head(kk, i), scalar=par2[:, C2_OML + i % 4:C2_OML + i % 4 + 1],
                                                   in1=head(e_, i), op0=ALU.mult, op1=ALU.mult).then_inc(keys, 1)
                dve.wait_ge(zmin, 1)
                dve.wait_ge(lns, 2)
                for i in range(8):
                    nc.vector.scalar_tensor_tensor(out=head(ng, i), in0=head(z, i), scalar=par2[:, C2_FLAG + i % 4:C2_FLAG + i % 4 + 1],
                                                   in1=head(ng, i), op0=ALU.mult, op1=ALU.add).then_inc(logf, 1)
                dve.wait_ge(logf, 8)
                nc.vector.tensor_tensor(ng, ng, l1, ALU.subtract).then_inc(logf, 1)
                dve.wait_ge(logf, 9)
                zb = z[:, HEADS * S:].rearrange("p (h s) -> p h s", h=HEADS)
                nc.vector.memset(zb[:, :, 0:1], 0.0).then_inc(csums, 1)
                for i in range(HEADS):
                    nc.vector.tensor_tensor_scan(head(z, i), ones_s, head(ng, i), 0.0, ALU.mult, ALU.add).then_inc(csums, 1)
                for i in range(HEADS):
                    nc.vector.tensor_tensor_scan(zb[:, i, 1:S], ones_s[:, 1:S], head(ng, HEADS + i)[:, 0:S - 1], 0.0,
                                                 ALU.mult, ALU.add).then_inc(csums, 1)
                dve.wait_ge(csums, 1 + 2 * HEADS)
                dve.wait_ge(keys, 8)

                def sides(t, h):
                    v = t.rearrange("p (n two i) -> p n two i", two=2, i=h)
                    return v[:, :, 0, :], v[:, :, 1, :]

                def exponents(l):
                    h = HALVES[l]
                    cl, cr = sides(z[:, 0:HEADS * S], h)
                    mid = cl[:, :, h - 1:h].broadcast_to(list(cl.shape))
                    if l >= 2:
                        dve.wait_ge(lev_mm, l - 1)
                    nc.vector.tensor_tensor(sides(LK[l % 2], h)[0], mid, cl, ALU.subtract)
                    nc.vector.tensor_tensor(sides(LQ[l % 2], h)[1], cr, mid, ALU.subtract).then_inc(sub_dve, 1)

                def level_queries(l):
                    if l == 0:
                        dve.wait_ge(hq_scaled, 1)
                    dve.wait_ge(lev_exp, 2 * l + 2)
                    nc.vector.tensor_tensor(LQ[l % 2], LQ[l % 2], hqT, ALU.mult).then_inc(mul_dve, 1)

                def merge(l):
                    dve.wait_ge(lev_mm, l + 1)
                    if l >= 2:
                        dve.wait_ge(merged, l)
                    for i in range(TT):
                        src = psum[:, 2 * (l % 2) + i, :].rearrange("p (h n) -> p h n", h=HEADS)
                        if l == 0:
                            last = nc.vector.tensor_copy(ST[:, i, 1 - i], src)
                        elif l == 1:
                            last = nc.vector.tensor_copy(ST[:, i, i], src)
                        else:
                            mask = masks2[:, (l - 2) * P:(l - 1) * P].unsqueeze(1).broadcast_to([P, HEADS, P])
                            last = nc.vector.copy_predicated(ST[:, i, i], mask, src)
                    last.then_inc(merged, 1)

                def rotate():
                    dve.wait_ge(const2_in, 16 * 2)
                    for i in range(4):
                        dve.wait_ge(proj2, 10 + i + 1)
                        if i >= 2:
                            dve.wait_ge(rotated, i - 1)
                        nc.vector.tensor_tensor(rot_t[:, i % 2], psum[:, 4 + (10 + i) % 4, :].rearrange("p (h s) -> p h s", h=2),
                                                table("sin").unsqueeze(1).broadcast_to([P, 2, S]), ALU.mult).then_inc(emp_dve, 1)
                        x2 = rqk[:, 512 * i:512 * (i + 1)].rearrange("p (h s) -> p h s", h=2)
                        nc.vector.tensor_tensor(x2, x2, table("cos").unsqueeze(1).broadcast_to([P, 2, S]),
                                                ALU.mult).then_inc(rot_cos, 1)
                        dve.wait_ge(emp_dve, i + 1)
                        dve.wait_ge(rot_cos, i + 1)
                        nc.vector.tensor_tensor(x2, x2, rot_t[:, i % 2], ALU.add).then_inc(rotated, 1)

                for it in range(LEVELS + 2):
                    if it < len(HALVES):
                        exponents(it)
                    if 1 <= it <= len(HALVES):
                        level_queries(it - 1)
                    if it >= 2:
                        merge(it - 2)
                    if it == 2:
                        rotate()
                for h in range(HEADS):
                    n = 22 + h
                    dve.wait_ge(proj2, n + 1)
                    src = psum[:, 4 + n % 4, :].rearrange("p (s n) -> p s n", s=TT)
                    for i in range(TT):
                        last = nc.vector.tensor_tensor(RS[:, h, i], src[:, i], table(f"decay{h}")[:, P - P * i:P - P * i + S],
                                                       ALU.mult)
                    last.then_inc(emp_dve, 1)
                dve.wait_ge(mix_rms, 1)
                dve.wait_ge(gated, 2)
                for t in range(TT):
                    nc.vector.scalar_tensor_tensor(out=XN[:, t, WIDTH:2 * WIDTH], in0=psum[:, t, :],
                                                   scalar=rsm[:, TT * HEADS + t:TT * HEADS + t + 1], in1=HG[:, t],
                                                   op0=ALU.mult, op1=ALU.mult)
                    for h in range(HEADS):
                        c = slice(h * HD, (h + 1) * HD)
                        last = nc.vector.scalar_tensor_tensor(out=XN[:, t, c], in0=psum[:, 2 + t, c],
                                                              scalar=rsm[:, t * HEADS + h:t * HEADS + h + 1], in1=RG[:, t, c],
                                                              op0=ALU.mult, op1=ALU.mult)
                    last.then_inc(mix_done, 1)
                turn_dve(dve, lay, 1, None)
                for i in range(4):
                    dve.wait_ge(wo_mm, i + 1)
                    dst = X[:, :, 256 * i:256 * (i + 1)]
                    nc.vector.tensor_tensor(dst, psum[:, 4 + i, :].rearrange("p (t n) -> p t n", t=TT), dst,
                                            ALU.add).then_inc(x_mid, 1)
                dve.wait_ge(x_mid, 4)
                norm_dve(dve, lay, 1)
                turn_dve(dve, lay, 2, par2[:, C2_N2:C2_N2 + 8])

                dve.wait_ge(logits, 1)
                lg = psum[:, 4, 0:TT * EXPERTS].rearrange("p (t e) -> p t e", t=TT)
                nc.vector.tensor_reduce(lmax, lg, AX.X, ALU.max).then_inc(soft, 1)
                dve.wait_ge(soft, 1)
                nc.vector.tensor_scalar(lmax, lmax, -1.0, None, ALU.mult).then_inc(soft, 1)
                nc.vector.memset(ones16, 1.0)
                dve.wait_ge(lexp, 1)
                nc.vector.reciprocal(linv, lsum).then_inc(soft, 1)
                dve.wait_ge(soft, 3)
                nc.vector.tensor_tensor(aff[:, :, :], elog[:, :, :], linv.unsqueeze(2).broadcast_to([P, TT, EXPERTS]),
                                        ALU.mult).then_inc(soft, 1)
                dve.wait_ge(affT_mm, 1)
                nc.vector.tensor_copy(left, psum[0:EXPERTS, 5, 0:S]).then_inc(top, 1)
                dve.wait_ge(top, 1)
                for r in range(CAP // 8):
                    nc.vector.max(top8[:, r, :], left).then_inc(top, 1)
                    dve.wait_ge(top, 2 * r + 2)
                    nc.vector.match_replace(left, top8[:, r, :], left, -1.0).then_inc(top, 1)
                    dve.wait_ge(top, 2 * r + 3)
                n = 1 + 2 * (CAP // 8)
                nc.vector.tensor_scalar(sel, left, 0.0, None, ALU.is_lt).then_inc(top, 1)
                dve.wait_ge(top, n + 1)
                nc.vector.tensor_tensor_scan(csum, ones16, sel, 0.0, ALU.mult, ALU.add).then_inc(top, 1)
                dve.wait_ge(top, n + 2)
                nc.vector.tensor_tensor(slotT, csum, sel, ALU.mult).then_inc(top, 1)
                dve.wait_ge(slot_mm, 1)
                nc.vector.tensor_copy(slot_of[:, :, :], psum[:, 4, 0:TT * EXPERTS].rearrange("p (t e) -> p t e", t=TT)).then_inc(top, 1)
                dve.wait_ge(top, n + 4)
                for t in range(TT):
                    nc.vector.tensor_tensor(ONE_HOT[:, t].rearrange("p (e c) -> p e c", c=CAP),
                                            slot_of[:, t].unsqueeze(2).broadcast_to([P, EXPERTS, CAP]),
                                            table("count").unsqueeze(1).broadcast_to([P, EXPERTS, CAP]),
                                            ALU.is_equal).then_inc(hot, 1)

                with dve.Fori(0, N_GROUPS) as g:
                    for b in range(2):
                        dve.wait_ge(xe_mm, b + 1)
                        nc.vector.tensor_tensor(XE[:, 4 * b:4 * b + 4, :], psum[:, b, :].rearrange("p (k n) -> p k n", k=4),
                                                par2[:, C2_N2 + 4 * b:C2_N2 + 4 * b + 4].unsqueeze(2).broadcast_to([P, 4, P]),
                                                ALU.mult).then_inc(xe_ready, 1)
                    for n in range(F_STEPS):
                        dve.wait_ge(g_silu, n + 1)
                        if n >= 2:
                            dve.wait_ge(hidT_mm, n - 1)
                        nc.vector.tensor_tensor(hid[:, n % 2], sg[:, n % 2], psum[:, 2 + n % 2, 256:512], ALU.mult).then_inc(g_hid, 1)
                    dve.wait_ge(dn_mm, F_STEPS)
                    nc.vector.tensor_copy(YE[:, 512:1024], psum[:, 7, :]).then_inc(ye_ready, 1)
                    for t in range(TT):
                        for c in range(2):
                            dve.wait_ge(sc_mm, 2 * t + c + 1)
                            dst = X[:, t, 512 * c:512 * (c + 1)]
                            nc.vector.tensor_tensor(dst, psum[:, 4 * t + c, :], dst, ALU.add).then_inc(x_moe, 1)
                    dve.wait_ge(x_moe, 4)
                    end_pass(dve, "dve")
                end_pass(dve, "dve")
            dve.wait_ge(fin_rms, 2 + 2)
            dve.wait_ge(fin_gain, 16 + 16)
            for t in range(TT):
                nc.vector.scalar_tensor_tensor(out=X[:, t], in0=X[:, t], scalar=rs[:, t:t + 1], in1=final_gain,
                                               op0=ALU.mult, op1=ALU.mult).then_inc(fin_done, 1)

        @block.tensor
        def _(pe):
            for s in range(SLOTS_1):
                pe.sem_inc(slot_free[s], 1)
            pe.wait_ge(s_small, SMALL)
            pe.wait_ge(s_rows, ROWS)
            for l in range(DEPTH):
                for i in range(2):
                    nc.tensor.transpose(psum[:, 2 * l + i, 0:P], rows[:, l, i, :], ident).then_inc(s_rowsT, 1)

            pending = []

            def release(over, value, uses):
                if pending:
                    last_over, last_value, last_uses = pending.pop()
                    pe.wait_ge(last_over, last_value)
                    for u in last_uses:
                        pe.sem_inc(slot_free[u % SLOTS], 1)
                if uses:
                    pending.append((over, value, uses))

            def wait_slot(lay, u, slots=SLOTS):
                s = u % slots
                pe.wait_ge(slot_loaded[s], 16)
                pe.sem_clear(slot_loaded[s])
                return slot(s)

            def columns_product(out, wt, c0, m):
                for k in range(KD):
                    last = nc.tensor.matmul(out, wt[:, k, c0:c0 + m], XT[:, k, :], start=(k == 0), stop=(k == KD - 1))
                return last

            def tokens_product(out, t, wt, c0, n):
                for k in range(KD):
                    last = nc.tensor.matmul(out, XT[:, k, t * P:(t + 1) * P], wt[:, k, c0:c0 + n],
                                            start=(k == 0), stop=(k == KD - 1))
                return last

            with pe.Fori(0, DEPTH) as lay:
                pe.wait_ge(xn_ready, TT)
                turn_pe(pe, lay, 0)
                turned_wait(pe, lay, 0)
                u = 0
                for i, (name, _, n) in enumerate(IN_BLOCKS):
                    wait_slot(lay, u, SLOTS_1)
                    wt = slot(u % SLOTS_1, 8 * n).rearrange("p (k n) -> p k n", k=8)
                    if i >= 4:
                        own = free_act if IN_OWNER[i - 4] == "act" else free_dve
                        pe.wait_ge(own, IN_COUNT[i - 4])
                    b = psum[:, 4 + i % 4, :]
                    if name in ("cq", "dv0", "dv1"):
                        for t in range(TT):
                            last = tokens_product(b[:, t * S:(t + 1) * S], t, wt, 0, 256)
                        last.then_inc(proj, 1)
                    elif name == "ckv":
                        for t in range(TT):
                            tokens_product(b[:, t * P:(t + 1) * P], t, wt, 0, KV_RANK)
                        columns_product(b[NOPE:MLA_QK, S:2 * S], wt, KV_RANK, ROPE).then_inc(proj, 1)
                    elif name == "fv":
                        for t in range(TT):
                            last = tokens_product(b[:, t * S:(t + 1) * S], t, wt, 0, 256)
                        last.then_inc(proj, 1)
                        pe.wait_ge(wu_loaded, 48)
                        columns_product(psum[0:FOX_H, 0, 0:S], wf, 0, FOX_H).then_inc(proj, 1)
                    else:
                        for m in range(2):
                            last = columns_product(b[:, m * S:(m + 1) * S], wt, m * P, P)
                        last.then_inc(proj, 1)
                    release(proj, i + 1 + (i >= 2), [u % SLOTS_1])
                    u += 1
                    if i == 5:
                        pe.wait_ge(free_dve, 2)
                        pe.wait_ge(fox_step, 1)
                        for k in range(2):
                            for t in range(TT):
                                last = nc.tensor.transpose(psum[:, 0, (2 * k + t) * P:(2 * k + t + 1) * P],
                                                           cqn[:, t, k * P:(k + 1) * P], ident)
                        last.then_inc(latT, 1)
                        for t in range(TT):
                            last = nc.tensor.transpose(psum[:, 1, t * P:(t + 1) * P], ckvn[:, t, :], ident)
                        last.then_inc(latT, 1)

                pe.wait_ge(lat_ready, 2)
                for b in range(2):
                    for h in range(2):
                        for k in range(2):
                            c = (2 * b + h) * MLA_QK
                            last = nc.tensor.matmul(psum[0:MLA_QK, 2 + b, h * S:(h + 1) * S], wuq[:, k, c:c + MLA_QK],
                                                    cqT[:, k, :], start=(k == 0), stop=(k == 1))
                    last.then_inc(mla_mm, 1)
                for b in range(2):
                    for h in range(2):
                        c = (2 * b + h) * (NOPE + MLA_V)
                        last = nc.tensor.matmul(psum[0:NOPE, b, h * S:(h + 1) * S], wukv[:, c:c + NOPE], ckvT,
                                                start=True, stop=True)
                    last.then_inc(mla_mm, 1)
                pe.wait_ge(free_dve, N_DVE_IN)
                pe.wait_ge(free_act, N_ACT_IN)
                wv = wukv.rearrange("p (h n) -> p h n", h=MLA_H)[:, :, NOPE:NOPE + MLA_V]
                for t in range(TT):
                    last = nc.tensor.matmul(psum[:, 4, t * S:(t + 1) * S], ckvT[:, t * P:(t + 1) * P], wv,
                                            start=True, stop=True)
                last.then_inc(mla_mm, 1)
                pe.wait_ge(s_tables, 16)
                at = where1["turn"][0]
                nc.tensor.matmul(psum[NOPE:MLA_QK, 5, 0:S], cst[NOPE:MLA_QK, at + NOPE:at + MLA_QK], kr,
                                 start=True, stop=True).then_inc(mla_mm, 1)

                def turn_queries():
                    for b in range(2):
                        pe.wait_ge(mla_q, b + 1)
                        for h in range(2):
                            last = nc.tensor.matmul(psum[0:MLA_QK, 6 + b, h * S:(h + 1) * S], const("turn", MLA_QK),
                                                    mqr[0:MLA_QK, 2 * b + h, :], start=True, stop=True)
                        last.then_inc(mla_turn, 1)

                turn_queries()
                pe.wait_ge(mla_kv, 3)
                pe.wait_ge(mla_rot, 2)

                def scores(j):
                    g, h, i = UNITS[j]
                    if j >= 2:
                        pe.wait_ge(biased, 2 * (j - 1))
                    if g == "diff":
                        q, k = dqT[64 * i:64 * i + 64, h, :], dkT[64 * i:64 * i + 64, h, :]
                    elif g == "fox":
                        a = 64 * (h % 2)
                        q, k = fqT[a:a + 64, h // 2, :], fkT[a:a + 64, h // 2, :]
                    else:
                        q, k = mq[0:MLA_QK, h, :], mk[0:MLA_QK, h, :]
                    if (g, h) == ("mla", 0):
                        pe.wait_ge(mla_rot, 6)
                    if (g, h) == ("fox", 0):
                        pe.wait_ge(fox_cum, 3)
                    for t, (a, b) in enumerate(((0, P), (P, SPAN))):
                        dst = psum[:, j % 2, a:b]
                        last = nc.tensor.matmul(dst, q[:, t * P:(t + 1) * P], k[:, 0:b - a], start=True, stop=(g != "fox"))
                        if g == "fox":
                            at = where1["pick"][0] + h * S
                            pick = cst[0:FOX_H, at:at + S]
                            nc.tensor.matmul(dst, ncum[:, t * P:(t + 1) * P], pick[:, 0:b - a], start=False, stop=False)
                            last = nc.tensor.matmul(dst, pick[:, 0:P], cum[:, 0:b - a], start=False, stop=True)
                    last.then_inc(scored, 1)

                def turn_probs(j):
                    pe.wait_ge(probs, j + 1)
                    if j >= 2:
                        pe.wait_ge(p_copied, j - 1)
                    for c in range(3):
                        last = nc.tensor.transpose(psum[:, 2 + j % 2, c * P:(c + 1) * P], sc[:, j % 3, c * P:(c + 1) * P], ident)
                    last.then_inc(p_turned, 1)

                def mix_values(j):
                    g, h, i = UNITS[j]
                    n = DIFF_V if g == "diff" else 64
                    v = {"diff": dv, "fox": fv, "mla": mv}[g][:, :, h * n:(h + 1) * n]
                    pe.wait_ge(p_copied, j + 1)
                    if j >= 2:
                        pe.wait_ge(out_done, j - 1)
                    o = psum[:, 4 + j % 2, :]
                    nc.tensor.matmul(o[:, 0:n], pT[:, j % 2, 0:P], v[:, 0], start=True, stop=True)
                    for t in range(TT):
                        last = nc.tensor.matmul(o[:, n:2 * n], pT[:, j % 2, (1 + t) * P:(2 + t) * P], v[:, t],
                                                start=(t == 0), stop=(t == 1))
                    last.then_inc(mixed, 1)

                for j in range(NU + 2):
                    if j < NU:
                        scores(j)
                    if 1 <= j <= NU:
                        turn_probs(j - 1)
                    if j >= 2:
                        mix_values(j - 2)

                pe.wait_ge(out_done, NU)
                pe.wait_ge(diff_done, 1)
                turn_pe(pe, lay, 1)
                turned_wait(pe, lay, 1)
                for i in range(4):
                    wt = wait_slot(lay, u, SLOTS_1).rearrange("p (k n) -> p k n", k=8)
                    for t in range(TT):
                        last = tokens_product(psum[:, 4 + i, t * S:(t + 1) * S], t, wt, 0, 256)
                    last.then_inc(wo_mm, 1)
                    release(wo_mm, i + 1, [u % SLOTS_1])
                    u += 1
                pe.wait_ge(xn_ready, 2 * TT)
                turn_pe(pe, lay, 2)
                release(None, 0, [])

                def split_ready(v):
                    pe.wait_ge(rest, v - FF_USE + 1)
                    pe.sem_inc(slot_free[v % SLOTS_1], 1)
                    return W1[(v - FF_USE) % W_BUFS][:, :], W2[(v - FF_USE) % W_BUFS][:, :]

                def up(j):
                    if j >= 2:
                        pe.wait_ge(conv, j - 1)
                    for g in range(2):
                        w1, w2 = (t.rearrange("p (k n) -> p k n", k=8) for t in split_ready(FF_OF[j, g]))
                        for m in range(2):
                            dst, c = psum[:, 4 + 2 * (j % 2) + g, m * S:(m + 1) * S], slice(m * P, (m + 1) * P)
                            for k in range(KD):
                                if j == g == m == 0:
                                    pe.wait_ge(xt_rest, k + 1)
                                nc.tensor.matmul(dst, w1[:, k, c], XT1[:, k, :], start=(k == 0), stop=False)
                                nc.tensor.matmul(dst, w1[:, k, c], XT2[:, k, :], start=False, stop=False)
                                last = nc.tensor.matmul(dst, w2[:, k, c], XT1[:, k, :], start=False, stop=(k == KD - 1))
                        last.then_inc(up_mm, 1)

                def down(j):
                    w1, w2 = (t.rearrange("p (k n) -> p k n", k=2) for t in split_ready(FF_OF[j, 2]))
                    pe.wait_ge(h_ready, j + 1)
                    for m in range(2):
                        for t in range(TT):
                            h1, h2 = (h[:, j % 2, m, t * P:(t + 1) * P] for h in (hT1, hT2))
                            for a, b in ((h1, w1), (h1, w2), (h2, w1)):
                                for c in range(2):
                                    last = nc.tensor.matmul(psum[:, 2 * t + c, :], a, b[:, m, 512 * c:512 * (c + 1)],
                                                            start=(j == 0 and m == 0 and b is w1 and a is h1),
                                                            stop=(j == FF_STEPS - 1 and m == 1 and a is h2))
                    last.then_inc(down_mm, 1)

                for j in range(FF_STEPS + 1):
                    if j < FF_STEPS:
                        up(j)
                    if j >= 1:
                        down(j - 1)
                end_pass(pe, "pe")
            pe.wait_ge(fin_gain, 16)
            for s in range(SLOTS_1, SLOTS):
                pe.sem_inc(slot_free[s], 1)

            with pe.Fori(0, DEPTH) as lay:
                pe.wait_ge(xn_ready, TT)
                turn_pe(pe, lay, 0)
                turned_wait(pe, lay, 0)

                def item(n):
                    kind, i = ITEMS[n]
                    bank = psum[:, 4 + n % 4, :]
                    if n >= 4:
                        owner, count = emptied_by(n - 4)
                        pe.wait_ge(emp_act if owner == "act" else emp_dve, count)
                    if kind == "in":
                        name = IN2_BLOCKS[i][0]
                        wt = wait_slot(lay, i).rearrange("p (k n) -> p k n", k=8)
                        for m in range(2):
                            dst = bank[:, m * S:(m + 1) * S]
                            if name[:2] in TOKEN_MAJOR:
                                last = tokens_product(dst, m, wt, 0, 256)
                            else:
                                last = columns_product(dst, wt, m * P, P)
                        last.then_inc(proj2, 1)
                        release(proj2, n + 1, [i])
                    elif kind == "rot":
                        if i == 0:
                            pe.wait_ge(const2_in, 16 * 2)
                            pe.wait_ge(emp_act, 10)
                        for h in range(2):
                            c = (2 * i + h) * S
                            last = nc.tensor.matmul(bank[:, h * S:(h + 1) * S], table("turn"), rqk[:, c:c + S],
                                                    start=True, stop=True)
                        last.then_inc(proj2, 1)
                    else:
                        if i == 0:
                            pe.wait_ge(rotated, 4)
                        for j in range(TT):
                            q, k = rqk[:, i * S:(i + 1) * S], rqk[:, (HEADS + i) * S + j * P:(HEADS + i) * S + (j + 1) * P]
                            last = nc.tensor.matmul(bank[:, j * S:(j + 1) * S], k, q, start=True, stop=True)
                        last.then_inc(proj2, 1)

                def level(l):
                    pe.wait_ge(mul_pool, l + 1)
                    if l < len(HALVES):
                        pe.wait_ge(mul_dve, l + 1)
                    if l >= 2:
                        pe.wait_ge(merged, l - 1)
                    lk, lq = heads(LK[l % 2]), heads(LQ[l % 2] if l < len(HALVES) else hqT)
                    for i in range(TT):
                        j = 1 - i if l == 0 else i
                        for h in range(HEADS):
                            last = nc.tensor.matmul(psum[:, 2 * (l % 2) + i, h * P:(h + 1) * P], lk[:, h, i * P:(i + 1) * P],
                                                    lq[:, h, j * P:(j + 1) * P], start=True, stop=True)
                    last.then_inc(lev_mm, 1)

                for n in range(22):
                    item(n)
                    if n >= 13:
                        level(n - 13)
                for n in range(22, 26):
                    item(n)
                pe.wait_ge(merged, LEVELS)
                for t in range(TT):
                    for h in range(HEADS):
                        for i in range(TT):
                            last = nc.tensor.matmul(psum[:, t, h * HD:(h + 1) * HD], ST[:, i, t, h, :],
                                                    hi[:, i, h * HD:(h + 1) * HD], start=(i == 0), stop=(i == 1))
                    last.then_inc(h_mixed, 1)
                pe.wait_ge(emp_dve, 8)
                for t in range(TT):
                    for h in range(HEADS):
                        for i in range(TT):
                            last = nc.tensor.matmul(psum[:, 2 + t, h * HD:(h + 1) * HD], RS[:, h, i, t * P:(t + 1) * P],
                                                    rv[:, i, h * HD:(h + 1) * HD], start=(i == 0), stop=(i == 1))
                    last.then_inc(r_mixed, 1)
                pe.wait_ge(mix_done, TT)
                turn_pe(pe, lay, 1)
                turned_wait(pe, lay, 1)
                for i in range(4):
                    wt = wait_slot(lay, 18 + i).rearrange("p (k n) -> p k n", k=8)
                    for t in range(TT):
                        last = tokens_product(psum[:, 4 + i, t * S:(t + 1) * S], t, wt, 0, 256)
                    last.then_inc(wo_mm, 1)
                    release(wo_mm, i + 1, [18 + i])
                pe.wait_ge(xn_ready, 2 * TT)
                turn_pe(pe, lay, 2)
                release(None, 0, [])
                turned_wait(pe, lay, 2)
                pe.wait_ge(small2, 16 * 3)
                for t in range(TT):
                    for k in range(KD):
                        last = nc.tensor.matmul(psum[:, 4, t * EXPERTS:(t + 1) * EXPERTS], XT[:, k, t * P:(t + 1) * P], wr[:, k, :],
                                                start=(k == 0), stop=(k == KD - 1))
                last.then_inc(logits, 1)
                pe.wait_ge(soft, 4)
                for t in range(TT):
                    last = nc.tensor.transpose(psum[0:EXPERTS, 5, t * P:(t + 1) * P], aff[:, t, :], ident)
                last.then_inc(affT_mm, 1)
                pe.wait_ge(top, 1 + 2 * (CAP // 8) + 3)
                for t in range(TT):
                    last = nc.tensor.transpose(psum[:, 4, t * EXPERTS:(t + 1) * EXPERTS], slotT[:, t * P:(t + 1) * P],
                                               ident[0:EXPERTS, 0:EXPERTS])
                last.then_inc(slot_mm, 1)
                pe.wait_ge(gated_hot, TT)
                for b in range(2):
                    for j in range(2):
                        for t in range(TT):
                            last = nc.tensor.transpose(psum[:, 6 + b, (2 * j + t) * P:(2 * j + t + 1) * P],
                                                       GATED[:, t, (2 * b + j) * P:(2 * b + j + 1) * P], ident)
                    last.then_inc(gt_mm, 1)
                pe.wait_ge(gt_ready, 2)

                with pe.Fori(0, N_GROUPS) as g:
                    pe.wait_ge(g_sel, 2)
                    for k in range(KD):
                        for t in range(TT):
                            last = nc.tensor.matmul(psum[:, k // 4, (k % 4) * P:(k % 4 + 1) * P], XN[:, t, k * P:(k + 1) * P],
                                                    pick_g[:, t, :], start=(t == 0), stop=(t == 1))
                        if k % 4 == 3:
                            last.then_inc(xe_mm, 1)

                    def gate_up(n):
                        if n == 0:
                            pe.wait_ge(xe_ready, 2)
                        if n >= 2:
                            pe.wait_ge(g_hid, n - 1)
                        for s in range(2 * GROUP):
                            pe.wait_ge(slot_loaded[s], 16)
                            pe.sem_clear(slot_loaded[s])
                        for k in range(KD):
                            for e in range(GROUP):
                                wt = ring[:, 2 * e * SLOT_W:(2 * e + 2) * SLOT_W].rearrange("p (m k n) -> p m k n", m=2, k=KD)
                                last = nc.tensor.matmul(psum[CAP * e:CAP * (e + 1), 2 + n % 2, :], XE[:, k, CAP * e:CAP * (e + 1)],
                                                        wt[:, :, k, :], start=(k == 0), stop=(k == KD - 1))
                        last.then_inc(gu_mm, 1)

                    def turn_hidden(n):
                        pe.wait_ge(g_hid, n + 1)
                        if n >= 2:
                            pe.wait_ge(hidT_ready, n - 1)
                        for i in range(2):
                            last = nc.tensor.transpose(psum[:, 4 + n % 2, i * P:(i + 1) * P], hid[:, n % 2, i * P:(i + 1) * P], ident)
                        last.then_inc(hidT_mm, 1)

                    def expert_down(n):
                        pe.wait_ge(hidT_ready, n + 1)
                        for s in range(2 * GROUP, 3 * GROUP):
                            pe.wait_ge(slot_loaded[s], 16)
                            pe.sem_clear(slot_loaded[s])
                        for i in range(2):
                            for c in range(2):
                                for e in range(GROUP):
                                    wt = slot(2 * GROUP + e).rearrange("p (i d) -> p i d", i=2)
                                    last = nc.tensor.matmul(psum[CAP * e:CAP * (e + 1), 6 + c, :],
                                                            hidT[:, n % 2, i, CAP * e:CAP * (e + 1)], wt[:, i, 512 * c:512 * (c + 1)],
                                                            start=(n == 0 and i == 0), stop=(n == F_STEPS - 1 and i == 1))
                        last.then_inc(dn_mm, 1)

                    for n in range(F_STEPS):
                        gate_up(n)
                        release(gu_mm, n + 1, list(range(2 * GROUP)))
                        release(None, 0, [])
                        turn_hidden(n)
                        expert_down(n)
                        release(dn_mm, n + 1, list(range(2 * GROUP, 3 * GROUP)))
                        release(None, 0, [])
                    release(None, 0, [])
                    pe.wait_ge(ye_ready, 2)
                    for t in range(TT):
                        for c in range(2):
                            nc.tensor.matmul(psum[:, 4 * t + c, :], gate_g[:, t * P:(t + 1) * P], YE[:, 512 * c:512 * (c + 1)],
                                             start=True, stop=True).then_inc(sc_mm, 1)
                    end_pass(pe, "pe")
                end_pass(pe, "pe")


NAMES = ["x", "ln1_g", "w_in", "fgate_b", "lam_q1", "lam_k1", "lam_q2", "lam_k2", "diff_norm_g", "q_norm_g", "w_uq",
         "kv_norm_g", "w_ukv", "w_o", "ln2_g", "w_up", "conv_w", "conv_b", "w_down", "final_g", "norm1_g_2", "w_in_2",
         "ret_norm_g_2", "hgrn_norm_g_2", "w_out_2", "lower_bounds_2", "norm2_g_2", "w_router_2", "w_gate_2",
         "w_up_2", "w_down_2", "final_norm_g_2"]


def kernel(**inputs):
    import concourse.bacc as bacc
    from concourse.bass_utils import run_bass_kernel_spmd

    nc = bacc.Bacc("TRN2", target_bir_lowering=False, num_devices=1)
    arrays, w = {}, {}
    for name in NAMES:
        a = np.ascontiguousarray(inputs[name])
        arrays[f"in_{name}"] = a
        w[name] = nc.dram_tensor(f"in_{name}", a.shape, mybir.dt.from_np(a.dtype), kind="ExternalInput").ap()
    out = nc.dram_tensor("out", (1, S, D), F32, kind="ExternalOutput").ap()
    build(nc, w, out)
    r = run_bass_kernel_spmd(nc, [arrays], core_ids=[0])
    return r.results[0]["out"]
```
